# Optimizing a Trainium2 kernel written in Bass

```python
import math
import jax, jax.numpy as jnp
from jax import lax
import numpy as np

D_MODEL = 1024
BATCH = 1
SEQ = 512
DEPTH = 1

HEAD_DIM = 64
N_META = 16
BLOCK = 128
NEG_INF = -1e30
SWA_WINDOW = 128
SWA_Q_HEADS = 8
SWA_KV_HEADS = 2
SWA_GROUP = SWA_Q_HEADS // SWA_KV_HEADS
FOX_HEADS = 8
LRU_WIDTH = D_MODEL // 2
LRU_BLOCKS = 8
LRU_BLOCK_DIM = LRU_WIDTH // LRU_BLOCKS
CONV_WIDTH = 4
LRU_C = 8.0
REL_BUCKETS = 32
REL_MAX_DIST = 128
D_FF = ((-(-8 * D_MODEL // 3)) + 255) // 256 * 256
N_BRANCH = 3
SPLIT_SIZES = (
    SWA_Q_HEADS * HEAD_DIM,
    SWA_KV_HEADS * HEAD_DIM,
    SWA_KV_HEADS * HEAD_DIM,
    FOX_HEADS * HEAD_DIM,
    FOX_HEADS * HEAD_DIM,
    FOX_HEADS * HEAD_DIM,
    FOX_HEADS,
    LRU_WIDTH,
    LRU_WIDTH,
    N_BRANCH * D_MODEL,
)
IN_COLS = sum(SPLIT_SIZES)


def rms_norm(x, g, eps=1e-6):
    xf = x.astype(jnp.float32)
    y = xf * lax.rsqrt(jnp.mean(xf * xf, axis=-1, keepdims=True) + eps)
    return (y * g.astype(jnp.float32)).astype(x.dtype)

def pad_left(a, n):
    return jnp.pad(a, [(0, 0), (n, 0)] + [(0, 0)] * (a.ndim - 2))

def t5_bucket(dist):
    max_exact = REL_BUCKETS // 2
    d = jnp.maximum(dist, 0)
    scaled = jnp.log(jnp.maximum(d, 1).astype(jnp.float32) / max_exact) / math.log(REL_MAX_DIST / max_exact)
    large = jnp.minimum(max_exact + (scaled * (REL_BUCKETS - max_exact)).astype(jnp.int32), REL_BUCKETS - 1)
    return jnp.where(d < max_exact, d, large)

def swa_sink_attention(q, k, v, sinks, rel_table, n_pad):
    b, tp, _, dh = q.shape
    nb = tp // BLOCK
    qb = q.reshape(b, nb, BLOCK, SWA_KV_HEADS, SWA_GROUP, dh)

    def band(a):
        a = a.reshape(b, nb, BLOCK, SWA_KV_HEADS, dh)
        prev = jnp.pad(a, ((0, 0), (1, 0), (0, 0), (0, 0), (0, 0)))[:, :-1]
        return jnp.concatenate([prev, a], axis=2)

    k_band, v_band = band(k), band(v)
    s = jnp.einsum('bnqhgd,bnkhd->bnhgqk', qb, k_band).astype(jnp.float32) * (dh ** -0.5)
    q_idx = jnp.arange(BLOCK)[:, None]
    k_idx = jnp.arange(2 * BLOCK)[None, :]
    dist = q_idx + BLOCK - k_idx
    bias = rel_table.astype(jnp.float32)[t5_bucket(dist)]
    bias = bias.transpose(2, 0, 1).reshape(SWA_KV_HEADS, SWA_GROUP, BLOCK, 2 * BLOCK)
    key_abs = (jnp.arange(nb)[:, None] - 1) * BLOCK + k_idx
    mask = ((dist >= 0) & (dist < SWA_WINDOW))[None] & (key_abs >= n_pad)[:, None, :]
    s = jnp.where(mask[None, :, None, None], s + bias, NEG_INF)
    sink = sinks.astype(jnp.float32).reshape(SWA_KV_HEADS, SWA_GROUP)[None, None, :, :, None, None]
    m = jnp.maximum(jnp.max(s, axis=-1, keepdims=True), sink)
    p = jnp.exp(s - m)
    denom = jnp.sum(p, axis=-1, keepdims=True) + jnp.exp(sink - m)
    p = (p / denom).astype(v.dtype)
    o = jnp.einsum('bnhgqk,bnkhd->bnqhgd', p, v_band)
    return o.reshape(b, tp, SWA_Q_HEADS * dh)

def forgetting_attention(q, k, v, log_f, n_pad):
    b, tp, h, dh = q.shape
    nb = tp // BLOCK
    cum = jnp.cumsum(log_f, axis=1).transpose(0, 2, 1)
    k_pos = jnp.arange(tp)
    qb = q.reshape(b, nb, BLOCK, h, dh).transpose(1, 0, 2, 3, 4)
    cb = cum.reshape(b, h, nb, BLOCK).transpose(2, 0, 1, 3)

    def one_block(args):
        qi, ci, n = args
        s = jnp.einsum('bqhd,bkhd->bhqk', qi, k).astype(jnp.float32) * (dh ** -0.5)
        s = s + ci[..., :, None] - cum[:, :, None, :]
        q_pos = n * BLOCK + jnp.arange(BLOCK)
        mask = (k_pos[None, :] <= q_pos[:, None]) & (k_pos >= n_pad)[None, :]
        s = jnp.where(mask, s, NEG_INF)
        p = jax.nn.softmax(s, axis=-1).astype(v.dtype)
        return jnp.einsum('bhqk,bkhd->bqhd', p, v)

    o = lax.map(one_block, (qb, cb, jnp.arange(nb)))
    return o.transpose(1, 0, 2, 3, 4).reshape(b, tp, h * dh)

def causal_depthwise_conv(x, w, bias):
    t = x.shape[1]
    xp = jnp.pad(x, ((0, 0), (CONV_WIDTH - 1, 0), (0, 0)))
    out = xp[:, 0:t] * w[0]
    for i in range(1, CONV_WIDTH):
        out = out + xp[:, i:i + t] * w[i]
    return out + bias

def rg_lru(x, w_r, b_r, w_i, b_i, lam):
    b, t, c = x.shape
    xb = x.reshape(b, t, LRU_BLOCKS, LRU_BLOCK_DIM)
    r = jax.nn.sigmoid(jnp.einsum('bthi,hij->bthj', xb, w_r).reshape(b, t, c).astype(jnp.float32) + b_r)
    gi = jax.nn.sigmoid(jnp.einsum('bthi,hij->bthj', xb, w_i).reshape(b, t, c).astype(jnp.float32) + b_i)
    log_a = LRU_C * r * jax.nn.log_sigmoid(lam.astype(jnp.float32))
    a = jnp.exp(log_a)
    inp = jnp.sqrt(-jnp.expm1(2.0 * log_a)) * (gi * x.astype(jnp.float32))

    def combine(left, right):
        a1, b1 = left
        a2, b2 = right
        return a1 * a2, a2 * b1 + b2

    _, h = lax.associative_scan(combine, (a, inp), axis=1)
    return h.astype(x.dtype)

def first_inputs(seed: int = 0) -> dict:
    key = jax.random.key(seed)
    ks = jax.random.split(key, 24)
    f32 = jnp.float32
    nrm = lambda k, shape, scale: jax.random.normal(k, shape, f32) * scale
    u = jax.random.uniform(ks[10], (DEPTH, LRU_WIDTH), f32, 0.9, 0.999)
    a0 = u ** (1.0 / LRU_C)
    return {
        "x": nrm(ks[0], (BATCH, SEQ, D_MODEL), 1.0),
        "meta_tokens": nrm(ks[1], (N_META, D_MODEL), 1.0),
        "rel_bias_table": nrm(ks[2], (REL_BUCKETS, SWA_Q_HEADS), 0.5),
        "norm_mix": 1.0 + nrm(ks[3], (DEPTH, D_MODEL), 0.02),
        "w_in": nrm(ks[4], (DEPTH, D_MODEL, IN_COLS), D_MODEL ** -0.5),
        "swa_sinks": nrm(ks[5], (DEPTH, SWA_Q_HEADS), 0.5),
        "fox_forget_bias": 2.0 + 3.0 * jax.random.uniform(ks[6], (DEPTH, FOX_HEADS), f32),
        "conv_w": nrm(ks[7], (DEPTH, CONV_WIDTH, LRU_WIDTH), CONV_WIDTH ** -0.5),
        "conv_b": nrm(ks[8], (DEPTH, LRU_WIDTH), 0.02),
        "lru_w_r": nrm(ks[9], (DEPTH, LRU_BLOCKS, LRU_BLOCK_DIM, LRU_BLOCK_DIM), LRU_BLOCK_DIM ** -0.5),
        "lru_b_r": nrm(ks[11], (DEPTH, LRU_WIDTH), 0.02),
        "lru_w_i": nrm(ks[12], (DEPTH, LRU_BLOCKS, LRU_BLOCK_DIM, LRU_BLOCK_DIM), LRU_BLOCK_DIM ** -0.5),
        "lru_b_i": nrm(ks[13], (DEPTH, LRU_WIDTH), 0.02),
        "lru_lambda": jnp.log(a0) - jnp.log1p(-a0),
        "w_branch": nrm(ks[14], (DEPTH, N_BRANCH, LRU_WIDTH, D_MODEL), LRU_WIDTH ** -0.5),
        "w_out": nrm(ks[15], (DEPTH, D_MODEL, D_MODEL), D_MODEL ** -0.5),
        "norm_ffn": 1.0 + nrm(ks[16], (DEPTH, D_MODEL), 0.02),
        "w_ffn_in": nrm(ks[17], (DEPTH, D_MODEL, 2 * D_FF), D_MODEL ** -0.5),
        "w_ffn_out": nrm(ks[18], (DEPTH, D_FF, D_MODEL), D_FF ** -0.5),
        "norm_final": 1.0 + nrm(ks[19], (D_MODEL,), 0.02),
    }

def first_block(x, meta_tokens, rel_bias_table, norm_mix, w_in, swa_sinks, fox_forget_bias, conv_w, conv_b,
              lru_w_r, lru_b_r, lru_w_i, lru_b_i, lru_lambda, w_branch, w_out, norm_ffn, w_ffn_in,
              w_ffn_out, norm_final):
    b = x.shape[0]
    meta = jnp.broadcast_to(meta_tokens.astype(x.dtype)[None], (b, N_META, D_MODEL))
    h = jnp.concatenate([meta, x], axis=1)
    t = h.shape[1]
    n_pad = (-t) % BLOCK
    split_points = [int(p) for p in np.cumsum(SPLIT_SIZES)[:-1]]
    for l in range(DEPTH):
        u = rms_norm(h, norm_mix[l])
        proj = u @ w_in[l]
        qa, ka, va, qf, kf, vf, fl, xc, yc, gates = jnp.split(proj, split_points, axis=-1)
        o_a = swa_sink_attention(
            pad_left(qa.reshape(b, t, SWA_Q_HEADS, HEAD_DIM), n_pad),
            pad_left(ka.reshape(b, t, SWA_KV_HEADS, HEAD_DIM), n_pad),
            pad_left(va.reshape(b, t, SWA_KV_HEADS, HEAD_DIM), n_pad),
            swa_sinks[l], rel_bias_table, n_pad)[:, n_pad:]
        log_f = jax.nn.log_sigmoid(fl.astype(jnp.float32) + fox_forget_bias[l].astype(jnp.float32))
        o_f = forgetting_attention(
            pad_left(qf.reshape(b, t, FOX_HEADS, HEAD_DIM), n_pad),
            pad_left(kf.reshape(b, t, FOX_HEADS, HEAD_DIM), n_pad),
            pad_left(vf.reshape(b, t, FOX_HEADS, HEAD_DIM), n_pad),
            pad_left(log_f, n_pad), n_pad)[:, n_pad:]
        xc = causal_depthwise_conv(xc, conv_w[l], conv_b[l])
        o_c = rg_lru(xc, lru_w_r[l], lru_b_r[l], lru_w_i[l], lru_b_i[l], lru_lambda[l]) * jax.nn.gelu(yc)
        g = jax.nn.sigmoid(gates).reshape(b, t, N_BRANCH, D_MODEL)
        merged = (g[:, :, 0] * (o_a @ w_branch[l, 0])
                  + g[:, :, 1] * (o_f @ w_branch[l, 1])
                  + g[:, :, 2] * (o_c @ w_branch[l, 2]))
        h = h + merged @ w_out[l]
        u = rms_norm(h, norm_ffn[l])
        gate_ff, up_ff = jnp.split(u @ w_ffn_in[l], 2, axis=-1)
        h = h + (jax.nn.silu(gate_ff) * up_ff) @ w_ffn_out[l]
    return rms_norm(h, norm_final)[:, N_META:]


M_HEADS = 4
M_HEAD_DIM = 128
M_WIDTH = M_HEADS * M_HEAD_DIM
CHUNK = 64
D_HEADS = 4
D_HEAD_DIM = 64
D_V_DIM = 2 * D_HEAD_DIM
D_WIDTH = D_HEADS * D_V_DIM
ROPE_THETA = 500000.0
ROPE_DIM = D_HEAD_DIM // 4
Q_BLOCK = 128
N_GROUPS = 4
EXPERTS_PER_GROUP = 8
N_EXPERTS = N_GROUPS * EXPERTS_PER_GROUP
TOP_K = 2
D_EXPERT = D_MODEL // 4
EPS = 1e-6
IN_SIZES = (M_WIDTH, M_WIDTH, M_WIDTH, M_WIDTH, M_HEADS, M_HEADS,
            D_WIDTH, D_WIDTH, D_WIDTH, D_MODEL, D_MODEL)
IN_COLS_2 = 4 * M_WIDTH + 2 * M_HEADS + 3 * D_WIDTH + 2 * D_MODEL


def rmsnorm(x, w):
    x32 = x.astype(jnp.float32)
    r = x32 * lax.rsqrt(jnp.mean(x32 * x32, axis=-1, keepdims=True) + EPS)
    return (r * w.astype(jnp.float32)).astype(x.dtype)

def to_heads(t, h):
    b, s, _ = t.shape
    return t.reshape(b, s, h, -1).transpose(0, 2, 1, 3)

def causal_conv(x, w, b):
    s = x.shape[1]
    xp = jnp.pad(x, ((0, 0), (CONV_WIDTH - 1, 0), (0, 0)))
    out = b
    for j in range(CONV_WIDTH):
        out = out + w[j] * xp[:, j:j + s]
    return out

def partial_rope(t, positions):
    inv_freq = ROPE_THETA ** (-jnp.arange(0, ROPE_DIM, 2, dtype=jnp.float32) / ROPE_DIM)
    ang = positions.astype(jnp.float32)[..., None] * inv_freq
    cos = jnp.cos(ang)[:, None, None].astype(t.dtype)
    sin = jnp.sin(ang)[:, None, None].astype(t.dtype)
    rot, rest = t[..., :ROPE_DIM], t[..., ROPE_DIM:]
    r1, r2 = jnp.split(rot, 2, axis=-1)
    rot = jnp.concatenate([r1 * cos - r2 * sin, r2 * cos + r1 * sin], axis=-1)
    return jnp.concatenate([rot, rest], axis=-1)

def mlstm_chunkwise(q, k, v, log_i, log_f):
    b_, h_, s_, d_ = q.shape
    nc = s_ // CHUNK
    chunks = lambda t: t.reshape(b_, h_, nc, CHUNK, *t.shape[3:]).transpose(2, 0, 1, 3, *range(4, t.ndim + 1))
    qc, kc, vc = chunks(q), chunks(k), chunks(v)
    ic, fc = chunks(log_i), chunks(log_f)
    causal = jnp.tril(jnp.ones((CHUNK, CHUNK), dtype=bool))

    def step(carry, inp):
        C, n, m = carry
        qt, kt, vt, it, ft = inp
        bcum = jnp.cumsum(ft, axis=-1)
        dmat = jnp.where(causal, bcum[..., :, None] - bcum[..., None, :] + it[..., None, :], -jnp.inf)
        m_inter = bcum + m[..., None]
        m_t = jnp.maximum(m_inter, jnp.max(dmat, axis=-1))
        s = jnp.einsum('bhtd,bhsd->bhts', qt, kt) * jnp.exp(dmat - m_t[..., None])
        inter = jnp.exp(m_inter - m_t)
        num = jnp.einsum('bhts,bhsd->bhtd', s, vt) + inter[..., None] * jnp.einsum('bhtk,bhkv->bhtv', qt, C)
        den = jnp.sum(s, axis=-1) + inter * jnp.einsum('bhtk,bhk->bht', qt, n)
        den = jnp.maximum(jnp.abs(den), jnp.exp(-m_t))
        h = num / den[..., None]
        b_last = bcum[..., -1]
        w = b_last[..., None] - bcum + it
        m_new = jnp.maximum(b_last + m, jnp.max(w, axis=-1))
        wexp = jnp.exp(w - m_new[..., None])
        decay = jnp.exp(b_last + m - m_new)
        C_new = decay[..., None, None] * C + jnp.einsum('bhs,bhsk,bhsv->bhkv', wexp, kt, vt)
        n_new = decay[..., None] * n + jnp.einsum('bhs,bhsk->bhk', wexp, kt)
        return (C_new, n_new, m_new), h

    init = (jnp.zeros((b_, h_, d_, d_), jnp.float32), jnp.zeros((b_, h_, d_), jnp.float32),
            jnp.zeros((b_, h_), jnp.float32))
    _, hs = lax.scan(step, init, (qc, kc, vc, ic, fc))
    return hs.transpose(1, 2, 0, 3, 4).reshape(b_, h_, s_, d_)

def diff_attention(q, k, v, lam):
    b_, h_, _, s_, d_ = q.shape
    nb = s_ // Q_BLOCK
    qb = q.reshape(b_, h_, 2, nb, Q_BLOCK, d_).transpose(3, 0, 1, 2, 4, 5)
    scale = d_ ** -0.5
    kpos = jnp.arange(s_)

    def block(args):
        qi, i = args
        sc = jnp.einsum('bhmqd,bhmkd->bhmqk', qi, k).astype(jnp.float32) * scale
        qpos = i * Q_BLOCK + jnp.arange(Q_BLOCK)
        sc = jnp.where(kpos[None, :] <= qpos[:, None], sc, -jnp.inf)
        p = jax.nn.softmax(sc, axis=-1)
        a = p[:, :, 0] - lam * p[:, :, 1]
        return jnp.einsum('bhqk,bhkd->bhqd', a.astype(v.dtype), v)

    out = lax.map(block, (qb, jnp.arange(nb)))
    return out.transpose(1, 2, 0, 3, 4).reshape(b_, h_, s_, v.shape[-1])

def hierarchical_moe(h, w_rg, b_rg, w_re, b_re, w_gate, w_up, w_down):
    b_, s_, d_ = h.shape
    hf = h.reshape(-1, d_)
    g_logits = (hf @ w_rg + b_rg).astype(jnp.float32)
    pg = jax.nn.softmax(g_logits, axis=-1)
    pg_top, g_idx = lax.top_k(pg, 1)
    e_logits = (hf @ w_re + b_re).astype(jnp.float32).reshape(-1, N_GROUPS, EXPERTS_PER_GROUP)
    e_sel = jnp.take_along_axis(e_logits, g_idx[:, :, None], axis=1)[:, 0]
    pe = jax.nn.softmax(e_sel, axis=-1)
    pe_top, j_idx = lax.top_k(pe, TOP_K)
    weights = pg_top * pe_top / jnp.sum(pe_top, axis=-1, keepdims=True)
    e_idx = g_idx * EXPERTS_PER_GROUP + j_idx
    combine = jnp.sum(jax.nn.one_hot(e_idx, N_EXPERTS, dtype=jnp.float32) * weights[..., None], axis=1)
    combine = combine.astype(h.dtype)
    y = jnp.zeros_like(hf)
    for e in range(N_EXPERTS):
        act = jax.nn.silu(hf @ w_gate[e]) * (hf @ w_up[e])
        y = y + combine[:, e:e + 1] * (act @ w_down[e])
    return y.reshape(b_, s_, d_)

def second_inputs(seed: int = 0) -> dict:
    key = jax.random.key(seed)
    ks = iter(jax.random.split(key, 40))
    nrm = lambda shape, s: jax.random.normal(next(ks), shape, jnp.float32) * s
    L = DEPTH
    x = nrm((BATCH, SEQ, D_MODEL), 1.0)
    c = nrm((BATCH, D_MODEL), 1.0)
    positions = (jnp.arange(SEQ, dtype=jnp.int32)[None, :]
                 + jax.random.randint(next(ks), (BATCH, 1), 0, 1024, dtype=jnp.int32))
    f_bias = jnp.broadcast_to(jnp.linspace(3.0, 6.0, M_HEADS, dtype=jnp.float32), (L, M_HEADS))
    return {
        "x": x, "c": c, "positions": positions,
        "w_ada": nrm((L, D_MODEL, 6 * D_MODEL), 0.5 * D_MODEL ** -0.5),
        "b_ada": nrm((L, 6 * D_MODEL), 0.02),
        "norm1_w": 1.0 + nrm((L, D_MODEL), 0.02),
        "w_in": nrm((L, D_MODEL, IN_COLS_2), D_MODEL ** -0.5),
        "b_igate": nrm((L, M_HEADS), 0.1),
        "b_fgate": f_bias + nrm((L, M_HEADS), 0.1),
        "conv_w": nrm((L, CONV_WIDTH, 2 * M_WIDTH), CONV_WIDTH ** -0.5),
        "conv_b": nrm((L, 2 * M_WIDTH), 0.02),
        "mlstm_norm_w": 1.0 + nrm((L, M_HEADS, M_HEAD_DIM), 0.02),
        "q_norm_w": 1.0 + nrm((L, D_HEAD_DIM), 0.02),
        "k_norm_w": 1.0 + nrm((L, D_HEAD_DIM), 0.02),
        "lam_q1": nrm((L, D_HEAD_DIM), 0.1),
        "lam_k1": nrm((L, D_HEAD_DIM), 0.1),
        "lam_q2": nrm((L, D_HEAD_DIM), 0.1),
        "lam_k2": nrm((L, D_HEAD_DIM), 0.1),
        "subln_w": 1.0 + nrm((L, D_V_DIM), 0.02),
        "w_br_m": nrm((L, M_WIDTH, D_MODEL), M_WIDTH ** -0.5),
        "w_br_d": nrm((L, D_WIDTH, D_MODEL), D_WIDTH ** -0.5),
        "w_out": nrm((L, D_MODEL, D_MODEL), D_MODEL ** -0.5),
        "norm2_w": 1.0 + nrm((L, D_MODEL), 0.02),
        "w_rg": nrm((L, D_MODEL, N_GROUPS), D_MODEL ** -0.5),
        "b_rg": nrm((L, N_GROUPS), 0.01),
        "w_re": nrm((L, D_MODEL, N_EXPERTS), D_MODEL ** -0.5),
        "b_re": nrm((L, N_EXPERTS), 0.01),
        "w_gate": nrm((L, N_EXPERTS, D_MODEL, D_EXPERT), D_MODEL ** -0.5),
        "w_up": nrm((L, N_EXPERTS, D_MODEL, D_EXPERT), D_MODEL ** -0.5),
        "w_down": nrm((L, N_EXPERTS, D_EXPERT, D_MODEL), D_EXPERT ** -0.5),
    }

def second_block(x, c, positions, w_ada, b_ada, norm1_w, w_in, b_igate, b_fgate, conv_w, conv_b,
              mlstm_norm_w, q_norm_w, k_norm_w, lam_q1, lam_k1, lam_q2, lam_k2, subln_w,
              w_br_m, w_br_d, w_out, norm2_w, w_rg, b_rg, w_re, b_re, w_gate, w_up, w_down):
    split_idx = [int(v) for v in np.cumsum(IN_SIZES)[:-1]]
    for l in range(DEPTH):
        mod = (c @ w_ada[l] + b_ada[l])[:, None, :]
        shift1, scale1, gate1, shift2, scale2, gate2 = jnp.split(mod, 6, axis=-1)

        h = rmsnorm(x, norm1_w[l]) * (1.0 + scale1) + shift1
        proj = h @ w_in[l]
        (q_m, k_m, v_m, o_m, i_pre, f_pre, q_d, k_d, v_d, g_m, g_d) = jnp.split(proj, split_idx, axis=-1)

        qk = jax.nn.silu(causal_conv(jnp.concatenate([q_m, k_m], axis=-1), conv_w[l], conv_b[l]))
        q_m, k_m = jnp.split(qk, 2, axis=-1)
        qh = to_heads(q_m, M_HEADS).astype(jnp.float32)
        kh = to_heads(k_m, M_HEADS).astype(jnp.float32) * (M_HEAD_DIM ** -0.5)
        vh = to_heads(v_m, M_HEADS).astype(jnp.float32)
        log_i = (i_pre + b_igate[l]).astype(jnp.float32).transpose(0, 2, 1)
        log_f = jax.nn.log_sigmoid((f_pre + b_fgate[l]).astype(jnp.float32)).transpose(0, 2, 1)
        hm = mlstm_chunkwise(qh, kh, vh, log_i, log_f).astype(x.dtype)
        hm = rmsnorm(hm.transpose(0, 2, 1, 3), mlstm_norm_w[l])
        hm = hm.reshape(x.shape[0], x.shape[1], M_WIDTH) * jax.nn.sigmoid(o_m)

        b_, s_ = x.shape[0], x.shape[1]
        qd = q_d.reshape(b_, s_, D_HEADS, 2, D_HEAD_DIM).transpose(0, 2, 3, 1, 4)
        kd = k_d.reshape(b_, s_, D_HEADS, 2, D_HEAD_DIM).transpose(0, 2, 3, 1, 4)
        qd = partial_rope(rmsnorm(qd, q_norm_w[l]), positions)
        kd = partial_rope(rmsnorm(kd, k_norm_w[l]), positions)
        vd = to_heads(v_d, D_HEADS)
        lam_init = 0.8 - 0.6 * math.exp(-0.3 * l)
        lam = (jnp.exp(jnp.sum(lam_q1[l] * lam_k1[l])) - jnp.exp(jnp.sum(lam_q2[l] * lam_k2[l]))
               + lam_init).astype(x.dtype)
        hd = diff_attention(qd, kd, vd, lam)
        hd = rmsnorm(hd.transpose(0, 2, 1, 3), subln_w[l]) * (1.0 - lam_init)
        hd = hd.reshape(b_, s_, D_WIDTH)

        merged = jax.nn.sigmoid(g_m) * (hm @ w_br_m[l]) + jax.nn.sigmoid(g_d) * (hd @ w_br_d[l])
        x = x + gate1 * (merged @ w_out[l])

        h2 = rmsnorm(x, norm2_w[l]) * (1.0 + scale2) + shift2
        x = x + gate2 * hierarchical_moe(h2, w_rg[l], b_rg[l], w_re[l], b_re[l],
                                         w_gate[l], w_up[l], w_down[l])
    return x


def setup_inputs(seed=0):
    out = dict(first_inputs(seed))
    for name, value in second_inputs(seed + 1).items():
        if name != "x":
            out[name + "_2"] = value
    return out


def reference(
    x, meta_tokens, rel_bias_table, norm_mix, w_in, swa_sinks, fox_forget_bias, conv_w, conv_b,
    lru_w_r, lru_b_r, lru_w_i, lru_b_i, lru_lambda, w_branch, w_out, norm_ffn, w_ffn_in,
    w_ffn_out, norm_final, c_2, positions_2, w_ada_2, b_ada_2, norm1_w_2, w_in_2, b_igate_2,
    b_fgate_2, conv_w_2, conv_b_2, mlstm_norm_w_2, q_norm_w_2, k_norm_w_2, lam_q1_2, lam_k1_2,
    lam_q2_2, lam_k2_2, subln_w_2, w_br_m_2, w_br_d_2, w_out_2, norm2_w_2, w_rg_2, b_rg_2,
    w_re_2, b_re_2, w_gate_2, w_up_2, w_down_2,
):
    x = first_block(
        x, meta_tokens, rel_bias_table, norm_mix, w_in, swa_sinks, fox_forget_bias, conv_w,
        conv_b, lru_w_r, lru_b_r, lru_w_i, lru_b_i, lru_lambda, w_branch, w_out, norm_ffn,
        w_ffn_in, w_ffn_out, norm_final,
    )
    return second_block(
        x, c_2, positions_2, w_ada_2, b_ada_2, norm1_w_2, w_in_2, b_igate_2, b_fgate_2,
        conv_w_2, conv_b_2, mlstm_norm_w_2, q_norm_w_2, k_norm_w_2, lam_q1_2, lam_k1_2,
        lam_q2_2, lam_k2_2, subln_w_2, w_br_m_2, w_br_d_2, w_out_2, norm2_w_2, w_rg_2, b_rg_2,
        w_re_2, b_re_2, w_gate_2, w_up_2, w_down_2,
    )


_drawn_inputs = setup_inputs


def setup_inputs(seed=0):
    import zlib

    import numpy as np

    out = dict(_drawn_inputs(seed))
    spreads = {}
    factors = {'norm_mix': 3.549,
     'swa_sinks': 64.0,
     'lru_b_r': 8.0,
     'lru_b_i': 8.0,
     'norm1_w_2': 4.739,
     'b_igate_2': 193.353,
     'conv_b_2': 52.608,
     'mlstm_norm_w_2': 18.208,
     'q_norm_w_2': 7.626,
     'k_norm_w_2': 8.0,
     'lam_q1_2': 50.616,
     'lam_k1_2': 50.544,
     'lam_q2_2': 8.0,
     'lam_k2_2': 6.194,
     'subln_w_2': 16.701,
     'b_rg_2': 20.962,
     'b_re_2': 26.088,
     'norm2_w_2': 4.766}
    for name, (base, spread) in spreads.items():
        noise = np.random.default_rng([zlib.crc32(name.encode()), seed]).standard_normal(out[name].shape)
        drawn = base * np.exp(spread * noise) if base else spread * noise
        out[name] = __import__('jax').numpy.asarray(drawn.astype(out[name].dtype))
    for name, factor in factors.items():
        out[name] = (out[name] * factor).astype(out[name].dtype)
    return out
```

```python
from contextlib import ExitStack

import numpy as np

import concourse.bass as bass
from concourse import mybir

F32 = mybir.dt.float32
F32R = mybir.dt.float32r
BF16 = mybir.dt.bfloat16
I32 = mybir.dt.int32
U32 = mybir.dt.uint32
ALU = mybir.AluOpType
ACT = mybir.ActivationFunctionType
AX_X = mybir.AxisListType.X

P = 128
D = 1024
KC = D // P
S = 512
M = 16
T = S + M
NB = S // P
DH = 64
W1 = 512
C1 = W1 // P
FF = 2816
FC = FF // P
NEG = -1e30
EPS = 1e-6
SLAB = 2048
RAW, HL = 3, 2
BAND = 2 * P
SKEW = 3 * P
NE = 32
NG = 4
EPG = NE // NG
DE = 256
NOV = (2 * S - 1) // P
NT = NE + NOV
UN = 3
TURNS = NE // UN + 1
LOST = -1e30

QA, KA, VA, QF, KF, VF, FL, XC, YC, GT = 0, 512, 640, 768, 1280, 1792, 2304, 2312, 2824, 3336
QM, KM, VM, OM, IF, QD, KD, VD, GM, GD = 0, 512, 1024, 1536, 2048, 2056, 2568, 3080, 3592, 4616

CW = dict(ident=P, halves=P, rope_swap=P, dist_mask=SKEW, inv_freq=1, onehot=SKEW, strict=P, expert=NE,
          token=NB)
CO = {}
_at = 0
for _k, _w in CW.items():
    CO[_k] = _at
    _at += _w
CTOT = _at


def constants():
    c = np.zeros((P, CTOT), np.float32)
    r = np.arange(P)
    c[:, CO["ident"]:CO["ident"] + P] = np.eye(P)
    c[:, CO["halves"]:CO["halves"] + P] = (r[:, None] // DH == r[None, :] // DH)
    for o in (0, DH):
        for j in range(8):
            c[o + 8 + j, CO["rope_swap"] + o + j] = -1.0
            c[o + j, CO["rope_swap"] + o + 8 + j] = 1.0
    dist = 2 * P - 1 - np.arange(SKEW)
    inside = (dist >= 0) & (dist < P)
    c[:, CO["dist_mask"]:CO["dist_mask"] + SKEW] = np.where(inside, 0.0, -NEG)
    d = np.clip(dist, 0, P - 1)
    scaled = (np.log(np.maximum(d, 1).astype(np.float32) / np.float32(16)) / np.float32(np.log(8.0))).astype(np.float32)
    bucket = np.where(d < 16, d, np.minimum(16 + (scaled * 16).astype(np.int32), 31))
    c[:32, CO["onehot"]:CO["onehot"] + SKEW] = (bucket[None] == np.arange(32)[:, None]) & inside
    freq = np.float32(500000.0) ** (-np.arange(0, 16, 2, dtype=np.float32) / np.float32(16))
    c[:, CO["inv_freq"]] = np.where(r % DH < 16, freq[r % 8], 0.0)
    c[:, CO["strict"]:CO["strict"] + P] = r[:, None] < r[None, :]
    c[:, CO["expert"]:CO["expert"] + NE] = np.arange(NE)
    c[:, CO["token"]:CO["token"] + NB] = np.arange(NB) * P + r[:, None]
    return c


ROWS_A = [("norm_mix", 8), ("conv_w", 16), ("conv_b", 4), ("lru_b_r", 4), ("lru_b_i", 4), ("lru_lambda", 4),
          ("norm_ffn", 8), ("norm_final", 8)]
ROWS_B = [("b_ada_2", 48), ("norm1_w_2", 8), ("conv_w_2", 32), ("conv_b_2", 8), ("mlstm_norm_w_2", 4),
          ("subln_w_2", 1), ("norm2_w_2", 8), ("c_2", 8), ("q_norm_w_2", 1), ("k_norm_w_2", 1)]


def column_of():
    at, col = 0, {}
    for rows, start in ((ROWS_A, 0), (ROWS_B, P)):
        at = start
        for name, n in rows:
            col[name] = at
            at += n
    return col


COL = column_of()


class Count:

    def __init__(self, sem):
        self.sem, self.n = sem, 0

    def __call__(self, ins, k=1):
        ins.then_inc(self.sem, k)
        self.n += k
        return self.n


def plan_dense():
    slabs, groups, bank_of, uses = [], {}, {}, [0] * 8
    turn = [0]

    def slab(name, kind, outs):
        n = len(slabs)
        gs = []
        for o in outs:
            if kind == "W" and name[0] == "ffo":
                b = o[1]
            else:
                b = turn[0] % 4
                turn[0] += 1
            bank_of[o] = (b, uses[b])
            uses[b] += 1
            groups[o] = len(groups)
            gs.append(o)
        slabs.append(dict(name=name, kind=kind, outs=gs, n=n))

    def feat(name, c0, n, meta):
        out = []
        for c in range(c0, c0 + n):
            out.append((name, c))
            if meta:
                out.append((name, c, "meta"))
        return out

    for i in range(2):
        slab(("xc", i), "W", feat("xc", 2 * i, 2, True))
    slab(("fl", 0), "W", feat("fl", 0, 1, True))
    for i in range(2):
        slab(("yc", i), "W", feat("yc", 2 * i, 2, False))
    for i in range(2):
        slab(("kf", i), "W", feat("kf", 2 * i, 2, True))
    for i in range(2):
        slab(("vf", i), "W", [("vf", i, t) for t in range(NB)] + [("vf", i, "meta")])
    for i in range(2):
        slab(("qf", i), "W", feat("qf", 2 * i, 2, False))
    for i in range(2):
        slab(("qa", i), "W", feat("qa", 2 * i, 2, False))
    slab(("kava", 0), "W", feat("ka", 0, 1, True) + [("va", 0, t) for t in range(NB)] + [("va", 0, "meta")])
    for b in range(3):
        for half in range(2):
            for q in range(2):
                slab(("gate", b, half, q), "W", feat(("gate", b), 4 * half + 2 * q, 2, False))
            slab(("branch", b, half), "W", feat(("branch", b), 4 * half, 4, False))
    for i in range(4):
        slab(("wo", i), "W", feat("wo", 2 * i, 2, False))
    n_ada = [0]

    def ada(n):
        for _ in range(n):
            slab(("ada", n_ada[0]), "A", [])
            n_ada[0] += 1

    for i in range(FC // 2):
        slab(("ffg", i), "W", feat("ffg", 2 * i, 2, False))
        ada(1)
        slab(("ffu", i), "W", feat("ffu", 2 * i, 2, False))
        ada(2 if i in (3, 6) else 1)
    for i in range(FC // 2):
        slab(("ffo", i), "W", feat("ffo", 0, 8, False) if i == FC // 2 - 1 else [])
    slab(("if", 0), "W", feat("if", 0, 1, False))
    for n in ("qm", "km", "vm", "om", "qd", "kd", "vd"):
        for i in range(2):
            if n in ("vm", "vd"):
                slab((n, i), "W", [(n, i, t) for t in range(NB)])
            else:
                slab((n, i), "W", feat(n, 2 * i, 2, False))
    for b in range(2):
        for half in range(2):
            for q in range(2):
                slab(("gate2", b, half, q), "W", feat(("gate2", b), 4 * half + 2 * q, 2, False))
            slab(("branch2", b, half), "W", feat(("branch2", b), 4 * half, 4, False))
    for i in range(4):
        slab(("wo2", i), "W", feat("wo2", 2 * i, 2, False))
    return slabs, groups, bank_of


SLABS, GROUPS, BANK = plan_dense()
SLAB_OF = {s["name"]: s for s in SLABS}
_h = _a = 0
for _s in SLABS:
    if _s["kind"] == "W":
        _s["h"] = _h
        _h += 1
    else:
        _s["a"] = _a
        _a += 1

W_SLABS = [s for s in SLABS if s["kind"] == "W"]


LRU_AFTER = [("kf", 0), ("kf", 1), ("vf", 0), ("vf", 1)]


def softmax_units(kind, tiles):
    units = []
    for pair in range(4):
        for side in range(2):
            h = 2 * pair + side if kind == "fox" else pair + 4 * side
            half = slice(DH * side, DH * side + DH)
            for i in range(NB):
                q = tiles["q"][half, pair, P * i:P * i + P]
                own = M + P * (i + 1)
                if kind == "fox":
                    first, band = 0, None
                    values = [(0, tiles["vm"][0:M, DH * h:DH * h + DH])]
                    values += [(M + P * j, tiles["v"][:, j, DH * h:DH * h + DH]) for j in range(i + 1)]
                    bias = tiles["bias"][:, h, 0:own]
                else:
                    first = 0 if i == 0 else own - BAND
                    vcol = slice(DH * side, DH * side + DH)
                    if i == 0:
                        values = [(0, tiles["vm"][0:M, vcol]), (M, tiles["v"][:, 0, vcol])]
                    else:
                        values = [(0, tiles["v"][:, i - 1, vcol]), (P, tiles["v"][:, i, vcol])]
                    bias = tiles["bias"][:, h, BAND - (own - first):BAND]
                keys = tiles["k"][half, pair, first:own] if kind == "fox" else tiles["k"][half, first:own]
                units.append(dict(n=len(units), pair=pair, side=side, i=i, h=h, q=q, k=keys, L=own - first,
                                  mask=(own - P) if kind == "fox" else None, bias=bias, values=values))
    return units


def shared_events():
    mean = dict(ms=1, root=1, rms=1)
    norm = dict(squared=KC, summed=KC, bc=1, **mean)
    split = dict(normed=KC, hi=KC, lo=KC)
    soft = dict(scored=32, exp=32, pt=32, pt_copied=32, pv=32, qk=32, p=32, out=4)
    families = [
        ("norm", [("n_ffn", dict(norm, **split)), ("n_fin", norm), ("n_one", dict(bc=1, **mean, **split)),
                  ("qk", dict(summed=8, bc=8, normed=8, **mean)),
                  ("mn", dict(squared=C1, summed=C1, bc=C1, **mean)),
                  ("dn", dict(squared=C1, summed=C1, bc=C1, **mean)), ("n_two", norm)]),
        ("softmax", [("fox", soft), ("swa", soft)]),
        ("merge", [("m1", dict(oh=3, ol=3, merged=2 * KC, hi=KC, lo=KC)),
                   ("m2", dict(oh=2, ol=2, merged=KC, hi=KC, lo=KC))]),
    ]
    out = {}
    for family, stages in families:
        before = {}
        for tag, events in stages:
            for event, n in events.items():
                out[f"{tag}_{event}"] = (f"{family}_{event}", before.get(event, 0))
                before[event] = before.get(event, 0) + n
    for chain, events in CHAINS.items():
        n = 0
        for event, count in events:
            out[event] = (chain, n)
            n += count
    return out


CHAINS = dict(
    act_steps=[("rms1", 2), ("identb_ready", 1), ("xt_copied", 8), ("umh_ready", 1), ("lam_exp", 1), ("forget_ln", 1),
               ("lru_tanh", 4), ("lru_sqrt", 4), ("cum_copied", 8), ("f_hi", FC), ("lam_exps", 1),
               ("if_ln", 1), ("if_g4", 1), ("if_ready", 1), ("sincos", 2), ("ml_absden", 4), ("df_out", 4),
               ("logits_copied", 1), ("group_exp", 1), ("h2t_even", 4), ("choice_exp", 1), ("xtm_even", 4), ("g2_even", 1), ("y1_scaled", 4)],
    dve_steps=[("xs_ready", 5), ("cols", 1), ("ul_ready", 8), ("um_ready", 1), ("uml_ready", 1),
               ("lam_abs", 1), ("lru_cols", 1), ("cols_b", 1), ("stage_ready", 8), ("conv_ready", 4), ("cum_ready", 2), ("lru_psum_read", 4), ("lru_done", 4),
               ("ada_summed", 24), ("mod_ready", 1), ("lam_prod", 2), ("h_final", 8), ("if_cum", 1),
               ("if_guard", 1), ("if_negm", 1), ("angles", 1), ("qk_roped", 8), ("ml_h", 4), ("ml_gated", 4), ("df_normed", 4),
               ("h2_ready", 8), ("slots_zero", 1), ("group_gap", 1), ("choice_gap", 1), ("choices", 1), ("slots_ready", 1),
               ("overflow_ready", 1), ("h2t_odd", 4), ("choice_weights", 1), ("xtm_odd", 4), ("g2_odd", 1), ("out_ready", 4)],
    pe_steps=[("col_mm", 1), ("us_ready", 8), ("um_mm", 1), ("col_b_mm", 1), ("dist_mm", 8),
              ("lru_mm", 4), ("cum_rows", 8), ("ada_used", 24),
              ("ffo_used", 10), ("lam_sums", 2), ("if_g", 1), ("if_cols", 1), ("qk_swap", 8), ("router_mm", 1), ("logits_ready", 1),
              ("token_major", 16), ("g2_mm", 1)],
    sp_moves=[("skew_written", 16), ("sbias_landed", 128), ("h2_stored", 64), ("out_stored", 64)],
    pool_moves=[("bd_landed", 64), ("pos_landed", 16), ("table_zeroed", 16), ("table_written", 128), ("table_landed", 16)],
)
SHARED = shared_events()


def build_program(nc, a, out):
    ctx = ExitStack()
    with ctx:
        sems, shared = {}, dict(SHARED)

        def S_(name):
            name = shared.get(name, (name, 0))[0]
            if name not in sems:
                sems[name] = ctx.enter_context(nc.semaphore(name))
            return sems[name]

        def when(name, value):
            return S_(name), shared.get(name, (name, 0))[1] + value

        base = (nc.sbuf_base + 63) // 64 * 64
        KB = 1024

        def at(name, kb, shape, dt=F32):
            return nc.alloc_sbuf_tensor_at(name, [P] + list(shape), dt, offset=int(base + kb * KB))[:]

        cst = at("cst", 0, [CTOT])
        pcol = at("pcol", 5.5, [2 * P])
        ones = at("ones", 6.5, [P])
        small = at("small", 7.0, [256])
        identb = at("identb", 8.0, [P], BF16)
        maskb = at("maskb", 8.25, [P], BF16)
        maskT = at("maskT", 9.5, [P])
        sinkb = at("sinkb", 8.5, [16])
        rel = at("rel", 8.5625, [8])
        fbias = at("fbias", 8.625, [4])
        mod = at("mod", 8.75, [48])
        rb = at("rb", 9.0, [36])
        stat = at("stat", 9.25, [64])
        hT = at("hT", 10, [KC, S])
        AH = at("AH", 26, [KC, S], F32R)
        AL = at("AL", 42, [KC, S], F32R)
        raw = at("raw", 58, [RAW, SLAB])
        WH = at("WH", 82, [HL, SLAB], F32R)
        WL = at("WL", 98, [HL, SLAB], F32R)
        W0 = 114
        xin = at("xin", W0, [NB, D])
        xs = at("xs", W0 + 16, [NB, D])
        xm = at("xm", W0 + 32, [D])
        xms = at("xms", W0 + 36, [D])
        rowsA = at("rowsA", W0 + 40, [P])
        rowsB = at("rowsB", W0 + 40.5, [P])
        QO = at("QO", W0, [3, C1, S])
        kf = at("kf", W0 + 24, [C1, T])
        ka = at("ka", W0 + 32.5, [T])
        va = at("va", W0 + 34.75, [NB, P])
        vam = at("vam", W0 + 36.75, [P])
        vf = at("vf", W0 + 37.25, [NB, W1])
        vfm = at("vfm", W0 + 45.25, [W1])
        AMH = at("AMH", W0 + 47.25, [KC, P], F32R)
        AML = at("AML", W0 + 51.25, [KC, P], F32R)
        Z0 = W0 + 55.25
        stage = at("stage", W0, [8, SKEW])
        utmp = at("utmp", Z0 + 12, [2, S])
        xc = at("xc", Z0, [C1, T])
        cv = at("cv", Z0 + 8.25, [C1, T])
        la = at("la", Z0 + 16.5, [C1, T])
        fl4 = at("fl4", Z0 + 24.75, [4, T])
        bd = at("bd", Z0 + 33, [2, C1, P])
        cbias = at("cbias", Z0, [8, T])
        Sb = at("Sb", Z0 + 16.5, [4, T])
        PT = at("PT", Z0 + 24.75, [2, 5 * P])
        sbias = at("sbias", Z0 + 29.75, [8, BAND])
        merged = at("merged", W0 + 24, [KC, S])
        OH = at("OH", W0 + 40, [C1, S], F32R)
        OL = at("OL", W0 + 48, [C1, S], F32R)
        gsig = at("gsig", W0 + 56, [4, S])
        FH = at("FH", W0, [FC, S], F32R)
        FL_ = at("FLo", W0 + 44, [FC, S], F32R)
        ftmp = at("ftmp", W0 + 88, [2, S])
        ntmp = at("ntmp", W0 + 64, [2, S])
        nrst = at("nrst", W0 + 68, [S])
        nout = at("nout", W0 + 70, [2, S])

        qkm = at("qkm", W0, [2, C1, S])
        om = at("om", W0 + 16, [C1, S])
        qkd = at("qkd", W0 + 24, [2, C1, S])
        vm = at("vm", W0 + 40, [NB, W1])
        vd = at("vd", W0 + 48, [NB, W1])
        cos = at("cos", W0 + 56, [S])
        sin = at("sin", W0 + 58, [S])
        ifr = at("ifr", W0 + 60, [7, S])
        mM = at("mM", W0 + 74, [S])
        mMd = at("mMd", W0 + 76, [S])
        mE = at("mE", W0 + 78, [2, S])
        mS = at("mS", W0 + 82, [2, S])
        rt = at("rt", W0 + 86, [3, S])
        posi = at("posi", W0 + 74, [S], I32)
        ang = at("ang", W0 + 76, [4, S])
        dP = at("dP", W0 + 60, [2, 2, S])
        dPT = at("dPT", W0 + 68, [2, S])
        gsig2 = at("gsig2", W0 + 40, [4, S])
        merged2 = at("merged2", W0 + 60, [KC, S])
        OH2 = at("OH2", W0 + 76, [C1, S], F32R)
        OL2 = at("OL2", W0 + 84, [C1, S], F32R)

        WE = at("WE", 26, [UN, KC * 2 * DE + 2 * D])
        Yt = at("Yt", 98, [UN, D])
        AT = at("AT", 110, [UN, 2 * P])
        xtm = at("xtm", W0, [NB, D])
        H2 = at("H2", W0 + 16, [KC, S])
        h2t = at("h2t", W0 + 32, [NB, D])
        g2row = at("g2row", W0 + 60, [D])
        Xg = at("Xg", W0 + 64, [UN, D])
        XT = at("XT", W0 + 76, [UN, KC * P])
        sA = at("sA", W0 + 88, [UN, DE])
        wr = at("wr", W0 + 92, [KC, NG + NE])
        yg = at("yg", 26, [2, NB, D])
        R0 = W0 + 48
        lgT = at("lgT", W0 + 72, [S])
        lg = at("lg", R0, [NB, NG + NE])
        gd = at("gd", R0 + 0.625, [NB, NG])
        ge = at("ge", R0 + 0.6875, [NB, NG])
        gc = at("gc", R0 + 0.75, [NB, NG])
        gh = at("gh", R0 + 0.8125, [NB, NG])
        r4 = at("r4", R0 + 0.875, [32, NB])
        em = at("em", R0 + 1.5, [NB, NE])
        cnd = at("cnd", R0 + 2, [NB, NE])
        ohs = at("ohs", R0 + 2.5, [2, NB, NE])
        both = at("both", R0 + 3.5, [NB, NE])
        prod = at("prod", R0 + 4, [2, NB, NE])
        eN = at("eN", R0 + 5, [4, NE])
        ovm = at("ovm", R0 + 5.5, [NOV, NE])
        later = at("later", R0 + 6.5, [NE])
        r8 = at("r8", R0 + 6.625, [10, 2, NB])
        eover = at("eover", R0 + 7, [NOV + 1], I32)
        slotix = at("slotix", R0 + 7.0625, [2, NB], U32)
        tid = at("tid", R0 + 7.125, [NB], U32)
        tok = at("tok", R0 + 7.25, [NT], U32)
        icol = at("icol", R0 + 7.5, [UN, 1], U32)
        zero = at("zero", R0 + 7.5625, [NT], U32)

        psum = ctx.enter_context(nc.psum_tensor("psum", [P, 8 * 512], F32))[:]

        def bank(b, n=512, at_=0):
            return psum[:, 512 * b + at_:512 * b + at_ + n]

        def K(name, w=None):
            return cst[:, CO[name]:CO[name] + (w or CW[name])]

        ident = K("ident")
        wsq = small[:, 208:224].rearrange("p (n j) -> p n j", j=2)
        ada_acc = [K("dist_mask", 256), K("onehot", 256)]

        def col(name, c=0, n=1):
            return pcol[:, COL[name] + c:COL[name] + c + n]

        h2_dram = nc.dram_tensor("h2_rows", (S, D), F32, kind="Internal").ap()
        tab_dram = nc.dram_tensor("token_of_slot", (P * NT, 1), U32, kind="Internal").ap()
        y_dram = nc.dram_tensor("expert_rows", (P * NT, D), F32, kind="Internal").ap()
        skew = nc.dram_tensor("skew", (P * 8 * SKEW,), F32, kind="Internal").ap()

        def slab_dmas(s, dst):
            name = s["name"]
            k, i = name[0], name[1]

            def kview(w, n, nk=KC):
                return dst[:, 0:nk * n].rearrange("p (k n) -> p k n", k=nk), w.rearrange("(k p) n -> p k n", p=P)

            def cols(w, c0, n):
                return [kview(w[:, c0:c0 + n], n)]

            w1, w2 = a["w_in"][0], a["w_in_2"][0]
            if k == "qa":
                res = []
                for hh in range(2):
                    for j in range(2):
                        h = 4 * j + 2 * i + hh
                        d_ = dst[:, 0:KC * 256].rearrange("p (k n) -> p k n", k=KC)[:, :, P * hh + DH * j:P * hh + DH * j + DH]
                        res.append((d_, w1[:, QA + DH * h:QA + DH * h + DH].rearrange("(k p) n -> p k n", p=P)))
                return res
            if k == "branch":
                _, b, half = name
                w = a["w_branch"][0, b][:, 512 * half:512 * half + 512]
                if b:
                    return [kview(w, 512, C1)]
                return [(dst[DH * j:DH * j + DH, :].rearrange("p (k n) -> p k n", k=C1),
                         w[256 * j:256 * j + 256, :].rearrange("(k p) n -> p k n", p=DH)) for j in range(2)]
            if k == "branch2":
                _, b, half = name
                return [kview(a["w_br_d_2" if b else "w_br_m_2"][0][:, 512 * half:512 * half + 512], 512, C1)]
            if k == "ffo":
                return [kview(a["w_ffn_out"][0][256 * i:256 * i + 256, :], D, 2)]
            if k == "gate":
                _, b, half, q = name
                return cols(w1, GT + D * b + 512 * half + 256 * q, 256)
            if k == "gate2":
                _, b, half, q = name
                return cols(w2, (GM, GD)[b] + 512 * half + 256 * q, 256)
            one = {"xc": XC, "yc": YC, "kf": KF, "vf": VF, "qf": QF}
            two = {"qm": QM, "km": KM, "vm": VM, "om": OM, "qd": QD, "kd": KD, "vd": VD}
            if k in one:
                return cols(w1, one[k] + 256 * i, 256)
            if k in two:
                return cols(w2, two[k] + 256 * i, 256)
            if k == "fl":
                return cols(w1, FL, P)
            if k == "if":
                return cols(w2, IF, P)
            if k == "kava":
                return cols(w1, KA, 256)
            if k == "wo":
                return cols(a["w_out"][0], 256 * i, 256)
            if k == "wo2":
                return cols(a["w_out_2"][0], 256 * i, 256)
            if k == "ada":
                return cols(a["w_ada_2"][0], 256 * i, 256)
            if k == "ffg":
                return cols(a["w_ffn_in"][0], 256 * i, 256)
            if k == "ffu":
                return cols(a["w_ffn_in"][0], FF + 256 * i, 256)
            raise ValueError(name)

        def width(s):
            return P * KC if s["name"][0] in ("fl", "if") else SLAB

        landed, _c = {}, [0] * RAW
        for s in SLABS:
            n = s["n"] % RAW
            _c[n] += 16 * len(slab_dmas(s, raw[:, n, :]))
            landed[s["n"]] = (n, _c[n])
        for u in range(UN):
            shared[f"gu_landed{u}"] = (f"raw_landed{u}", _c[u])

        def slab_consumed(eng, s):
            if s["outs"]:
                eng.wait_ge(*when("dense_ready", GROUPS[s["outs"][-1]] + 1))
            else:
                eng.wait_ge(*when("ffo_used", s["name"][1] + 1))

        def freed(eng, g):
            b, used = BANK[g]
            eng.wait_ge(*when(f"bank_free{b}", used + 1))

        def merged_at(eng, tag, it):
            if it < KC:
                freed(eng, (("branch" if tag == "m1" else "branch2", 0), it))
            else:
                eng.wait_ge(*when(tag + "_merged", it - KC + 1))

        gain = small[:, 72:80]
        shift1, scale1, gate1, shift2, scale2, gate2 = (mod[:, 8 * i:8 * i + 8] for i in range(6))

        fox = softmax_units("fox", dict(q=QO[:, 1], k=kf, v=vf, vm=vfm, bias=cbias))
        swa = softmax_units("swa", dict(q=QO[:, 0], k=ka, v=va, vm=vam, bias=sbias))

        block = ctx.enter_context(nc.Block())

        last_h = len(W_SLABS) - 1
        vec_dmas = []
        for rows, tile in ((ROWS_A, rowsA), (ROWS_B, rowsB)):
            r = 0
            for name, n in rows:
                v = a[name]
                if name in ("q_norm_w_2", "k_norm_w_2"):
                    vec_dmas += [(tile[r:r + 1, DH * j:DH * j + DH], v) for j in range(2)]
                else:
                    names = "abc"[:len(v.shape) - 1]
                    if names:
                        lhs = " ".join(names)
                        v = v.rearrange(f"{lhs} (r p) -> ({lhs} r) p", p=P)
                    else:
                        v = v.rearrange("(r p) -> r p", p=P)
                    vec_dmas.append((tile[r:r + n, :], v))
                r += n
        extra_dmas = [
            (rel[0:32, 0:8], a["rel_bias_table"]),
            (sinkb[:, 0:8], a["swa_sinks"][0].partition_broadcast(P)),
            (fbias[0:8, 0:1], a["fox_forget_bias"].rearrange("a h -> h a")),
            (fbias[0:4, 1:2], a["b_igate_2"].rearrange("a h -> h a")),
            (fbias[4:8, 1:2], a["b_fgate_2"].rearrange("a h -> h a")),
            (rb[:, 0:4], a["b_rg_2"][0].partition_broadcast(P)),
            (rb[:, 4:36], a["b_re_2"][0].partition_broadcast(P)),
        ] + [
            (small[0:DH, 64 + i:65 + i], a[n].rearrange("a d -> d a"))
            for i, n in enumerate(("lam_q1_2", "lam_k1_2", "lam_q2_2", "lam_k2_2"))
        ]
        PARAMS = 16 * (len(vec_dmas) - len(ROWS_A) + len(extra_dmas))

        def load_expert(sp, i, u, e):
            n = UN * i + u
            gate_up = WE[:, u, 0:KC * 2 * DE].rearrange("p (k n) -> p k n", k=KC)
            down = WE[:, u, KC * 2 * DE:].rearrange("p (k n) -> p k n", k=2)
            one = bass.ds(e, 1)
            if isinstance(i, int) and i == 0:
                sp.wait_ge(*when("dense_ready", len(GROUPS)))
            else:
                sp.wait_ge(*when("gu_done", n - (UN - 1)))
            for w, c0 in ((a["w_gate_2"], 0), (a["w_up_2"], DE)):
                sp.dma_start(gate_up[:, :, c0:c0 + DE].unsqueeze(1), w[0].rearrange("e (k p) n -> p e k n", p=P)[:, one]
                             ).then_inc(S_(f"gu_landed{u}"), 16)
            if not (isinstance(i, int) and i == 0):
                sp.wait_ge(*when("y_done", n - (UN - 1)))
            sp.dma_start(down.unsqueeze(1), a["w_down_2"][0].rearrange("e (k p) n -> p e k n", p=P)[:, one]
                         ).then_inc(S_(f"down_landed{u}"), 16)

        choice_gap, choice_exp, weight1, weight2 = (r4[:, n, :] for n in (0, 1, 2, 3))

        def turn(step, i, first=False, last=False):
            for u in range(UN):
                ahead = None if last and u == UN - 1 else (i + (u + 1) // UN, (u + 1) % UN)
                before = None if first and u == 0 else (i - 1, UN - 1) if u == 0 else (i, u - 1)
                step(i, u, ahead, before)

        def run_tiles(eng, step):
            turn(step, 0, first=True)
            with eng.Fori(1, TURNS - 1) as i:
                turn(step, i)
            turn(step, TURNS - 1, last=True)

        def run_overflow(step):
            for i in range(TURNS, NT // UN):
                turn(step, i, first=i == TURNS, last=i == NT // UN - 1)

        def more_tiles(eng):
            eng.wait_ge(*when("overflow_ready", 1))
            return eng.value_load(eover[0:1, NOV:NOV + 1], min_val=0, max_val=NOV) > UN * TURNS - NE

        @block.sync
        def _(sp):
            for t in range(NB):
                sp.dma_start(xin[:, t, :], a["x"][0, P * t:P * t + P, :]).then_inc(S_(f"x_landed{t}"), 16)
            sp.dma_start(xm[0:M, :], a["meta_tokens"]).then_inc(S_("meta_landed"), 16)
            sp.dma_start(cst, a["const"]).then_inc(S_("cst_landed"), 16)
            for dst, src in vec_dmas[:len(ROWS_A)]:
                sp.dma_start(dst, src).then_inc(S_("rows_landed"), 16)
            for s in SLABS:
                n = s["n"]
                if n >= RAW:
                    old = SLABS[n - RAW]
                    if old["kind"] == "W":
                        sp.wait_ge(*when("lo_ready", old["h"] + 1))
                    else:
                        sp.wait_ge(*when("ada_summed", old["a"] + 1))
                for dst, src in slab_dmas(s, raw[:, n % RAW, :]):
                    sp.dma_start(dst, src).then_inc(S_(f"raw_landed{n % RAW}"), 16)
                if s["name"] == ("fl", 0):
                    sp.wait_ge(*when("stage_ready", 8))
                    sp.dma_start(skew.rearrange("(p n) -> p n", p=P), stage.rearrange("p h n -> p (h n)")
                                 ).then_inc(S_("skew_written"), 16)
                if s["name"] == ("qa", 1):
                    sp.wait_ge(*when("skew_written", 16))
                    sp.wait_ge(*when("cum_copied", 8))
                    lines = skew[P - 1:P - 1 + P * (8 * SKEW - 1)].rearrange("(p n) -> p n", p=P)
                    for h in range(8):
                        sp.dma_start(sbias[:, h, :], lines[:, SKEW * h:SKEW * h + BAND]).then_inc(S_("sbias_landed"), 16)
            for u in range(UN):
                load_expert(sp, 0, u, u)
            for t in range(NB):
                sp.wait_ge(*when("h2t_even", t + 1))
                sp.wait_ge(*when("h2t_odd", t + 1))
                sp.dma_start(h2_dram[P * t:P * t + P, :], h2t[:, t, :]).then_inc(S_("h2_stored"), 16)
            def store_tile(i, u):
                sp.wait_ge(*when("y_even", UN * i + u + 1))
                sp.wait_ge(*when("y_odd", UN * i + u + 1))
                rows = y_dram.rearrange("(p t) n -> p t n", t=NT)
                sp.dma_start(rows[:, bass.ds(UN * i + u, 1), :], Yt[:, u, :].unsqueeze(1)).then_inc(S_(f"y_stored{u}"), 16)

            with sp.Fori(1, NE // UN) as i:
                for u in range(UN):
                    load_expert(sp, i, u, UN * i + u)
                    store_tile(i - 1, u)

            def expert_of(n):
                if n < NE:
                    return n
                if n == NE:
                    sp.wait_ge(*when("overflow_ready", 1))
                return sp.value_load(eover[0:1, n - NE:n - NE + 1], min_val=0, max_val=NE - 1)

            for u in range(UN):
                load_expert(sp, TURNS - 1, u, expert_of(UN * (TURNS - 1) + u))
                store_tile(TURNS - 2, u)
            for u in range(UN):
                store_tile(TURNS - 1, u)
            with sp.If(more_tiles(sp)):
                sp.wait_ge(*when("spare_written", 16))
                for n in range(UN * TURNS, NT):
                    load_expert(sp, n // UN, n % UN, expert_of(n))
                    if n >= UN * (TURNS + 1):
                        store_tile(n // UN - 1, n % UN)
                for u in range(UN):
                    store_tile(NT // UN - 1, u)
            for t in range(NB):
                sp.wait_ge(*when("out_ready", t + 1))
                sp.dma_start(out[0, P * t:P * t + P, :], xtm[:, t, :]).then_inc(S_("out_stored"), 16)
            sp.wait_ge(*when("out_stored", 16 * NB))

        @block.gpsimd
        def _(pool):
            nc.gpsimd.memset(ones, 1.0).then_inc(S_("pool_set"), 1)
            nc.gpsimd.memset(AMH.bitcast(F32), 0.0).then_inc(S_("pool_set"), 1)
            nc.gpsimd.memset(AML.bitcast(F32), 0.0).then_inc(S_("pool_set"), 1)
            nc.gpsimd.memset(maskb, 0.0).then_inc(S_("pool_set"), 1)
            nc.gpsimd.memset(bd, 0.0).then_inc(S_("pool_set"), 1)
            nc.gpsimd.memset(small[:, 255:256], EPS).then_inc(S_("pool_set"), 1)
            for dst, src in vec_dmas[len(ROWS_A):] + extra_dmas:
                pool.dma_start(dst, src).then_inc(S_("params"), 16)
            pool.wait_ge(*when("pool_set", 6))
            nc.gpsimd.affine_select(out=maskb, in_=maskb, compare_op=ALU.is_ge, fill=-NEG, base=0,
                                    pattern=[[-1, P]], channel_multiplier=1).then_inc(S_("pool_set"), 1)
            for g, w in enumerate(("lru_w_r", "lru_w_i")):
                for j in range(2):
                    pool.dma_start(bd[DH * j:DH * j + DH, g, :, DH * j:DH * j + DH],
                                   a[w][0].rearrange("(c j) i o -> j i c o", j=2)[j]).then_inc(S_("bd_landed"), 16)
            pool.wait_ge(*when("cst_landed", 16))
            spare = NT - UN * TURNS
            pool.dma_start(y_dram.rearrange("(p t) n -> p t n", t=NT)[:, UN * TURNS:, :],
                           cst[:, 0:D].unsqueeze(1).to_broadcast([P, spare, D])).then_inc(S_("spare_written"), 16)
            nc.gpsimd.memset(maskT, 0.0).then_inc(S_("pool_set"), 1)
            pool.wait_ge(*when("pool_set", 8))
            nc.gpsimd.affine_select(out=maskT, in_=maskT, compare_op=ALU.is_ge, fill=NEG, base=0,
                                    pattern=[[1, P]], channel_multiplier=-1).then_inc(S_("pool_set"), 1)

            for n in range(KC):
                freed(pool, ("ffo", n))
            pool.dma_start(posi, a["positions_2"][0].partition_broadcast(P)).then_inc(S_("pos_landed"), 16)
            for w, c0, n in ((a["w_rg_2"], 0, NG), (a["w_re_2"], NG, NE)):
                pool.dma_start(wr[:, :, c0:c0 + n], w[0].rearrange("(k p) n -> p k n", p=P)).then_inc(S_("router_landed"), 16)
            pool.wait_ge(*when("slots_zero", 1))
            pool.dma_start(tab_dram.rearrange("(p t) o -> p (t o)", t=NT), zero).then_inc(S_("table_zeroed"), 16)
            pool.wait_ge(*when("table_zeroed", 16))
            pool.wait_ge(*when("slots_ready", 1))
            for c in range(2):
                for t in range(NB):
                    pool.indirect_dma_start(out=tab_dram, out_offset=bass.IndirectOffsetOnAxis(ap=slotix[:, c, t:t + 1], axis=0),
                                            in_=tid[:, t:t + 1], in_offset=None).then_inc(S_("table_written"), 16)
            pool.wait_ge(*when("table_written", 16 * 2 * NB))
            pool.dma_start(tok, tab_dram.rearrange("(p t) o -> p (t o)", t=NT)).then_inc(S_("table_landed"), 16)
            pool.wait_ge(*when("h2_stored", 16 * NB))

            def gather(i, u):
                n = UN * i + u
                if not (isinstance(i, int) and i == 0):
                    pool.wait_ge(*when("tx_done", n - (UN - 1)))
                pool.wait_ge(*when("icol_ready", n + 1))
                pool.sem_inc(S_("gathers"), 1)
                pool.indirect_dma_start(out=Xg[:, u, :], out_offset=None, in_=h2_dram,
                                        in_offset=bass.IndirectOffsetOnAxis(ap=icol[:, u, :], axis=0)
                                        ).then_inc(S_(f"xg_landed{u}"), 16)

            for u in range(UN):
                gather(0, u)
            with pool.Fori(1, TURNS) as i:
                for u in range(UN):
                    gather(i, u)
            pool.wait_ge(*when("spare_written", 16))
            with pool.If(more_tiles(pool)):
                for n in range(UN * TURNS, NT):
                    gather(n // UN, n % UN)
                for u in range(UN):
                    pool.wait_ge(*when(f"y_stored{u}", 16 * (NT // UN)))
            for u in range(UN):
                pool.wait_ge(*when(f"y_stored{u}", 16 * TURNS))
            for t in range(NB):
                for c in range(2):
                    pool.indirect_dma_start(out=yg[:, c, t, :], out_offset=None, in_=y_dram,
                                            in_offset=bass.IndirectOffsetOnAxis(ap=slotix[:, c, t:t + 1], axis=0)
                                            ).then_inc(S_(f"yg_landed{t}"), 16)

        eps = small[:, 255:256]
        units_of = {"fox": fox, "swa": swa}

        @block.scalar
        def _(act):
            chain = Count(S_("act_chain"))

            def link(ins):
                chain(ins)
                act.wait_ge(chain.sem, chain.n)

            fed = [0]

            def feed(h):
                while fed[0] <= min(h, last_h):
                    s = W_SLABS[fed[0]]
                    sem, value = landed[s["n"]]
                    act.wait_ge(*when(f"raw_landed{sem}", value))
                    if fed[0] >= HL:
                        slab_consumed(act, W_SLABS[fed[0] - HL])
                        act.wait_ge(*when("lo_ready", fed[0] - HL + 1))
                    w = width(s)
                    nc.scalar.activation(WH[:, fed[0] % HL, 0:w], raw[:, s["n"] % RAW, 0:w], ACT.Copy
                                         ).then_inc(S_("hi_ready"), 1)
                    fed[0] += 1

            def ready(g):
                act.wait_ge(*when("dense_ready", GROUPS[g] + 1))
                return bank(BANK[g][0])

            def free(g, ins):
                ins.then_inc(S_(f"bank_free{BANK[g][0]}"), 1)

            for t in range(NB):
                act.wait_ge(*when(f"x_landed{t}", 16))
                if t == 0:
                    link(nc.scalar.activation(xs[:, t, :], xin[:, t, :], ACT.Square, accum_out=stat[:, t:t + 1]))
                else:
                    nc.scalar.activation(xs[:, t, :], xin[:, t, :], ACT.Square, accum_out=stat[:, t:t + 1]
                                         ).then_inc(S_("act_chain"), 1)
                    chain.n += 1
            act.wait_ge(*when("meta_landed", 16))
            link(nc.scalar.activation(xms[0:M, :], xm[0:M, :], ACT.Square, accum_out=stat[0:M, 4:5]))
            act.wait_ge(*when("pool_set", 6))
            nc.scalar.activation(stat[:, 8:12], stat[:, 0:4], ACT.Sqrt, bias=eps, scale=1.0 / D).then_inc(S_("rms1"), 1)
            nc.scalar.activation(stat[0:M, 12:13], stat[0:M, 4:5], ACT.Sqrt, bias=eps[0:M], scale=1.0 / D
                                 ).then_inc(S_("rms1"), 1)
            feed(0)
            act.wait_ge(*when("cst_landed", 16))
            nc.scalar.activation(identb, ident, ACT.Copy).then_inc(S_("identb_ready"), 1)
            feed(1)
            for u in range(2 * NB):
                t, half = u // 2, u % 2
                act.wait_ge(*when("xt_ready", u + 1))
                nc.scalar.activation(hT[:, 4 * half:4 * half + 4, P * t:P * t + P],
                                     bank(4 + u % 2).rearrange("p (k n) -> p k n", k=4), ACT.Copy
                                     ).then_inc(S_("xt_copied"), 1)
                act.wait_ge(*when("un_ready", u + 1))
                nc.scalar.activation(AH[:, 4 * half:4 * half + 4, P * t:P * t + P],
                                     utmp[:, u % 2, :].rearrange("p (k n) -> p k n", k=4), ACT.Copy
                                     ).then_inc(S_("uh_ready"), 1)
            act.wait_ge(*when("um_ready", 1))
            nc.scalar.activation(AMH[:, :, 0:M], utmp[:, 0, 0:KC * M].rearrange("p (k n) -> p k n", k=KC), ACT.Copy
                                 ).then_inc(S_("umh_ready"), 1)

            act.wait_ge(*when("lam_abs", 1))
            nc.scalar.activation(small[:, 36:40], small[:, 32:36], ACT.Exp, scale=-1.0).then_inc(S_("lam_exp"), 1)


            def copy_out(g, dst, src, scale=1.0, func=ACT.Copy):
                nc.scalar.activation(dst, src, func, scale=scale).then_inc(S_(f"bank_free{BANK[g][0]}"), 1)

            def lru_gates(c):
                act.wait_ge(*when("lru_cols", 1))
                act.wait_ge(*when("lru_mm", c + 1))
                r, g = psum[:, 2048:2048 + T], psum[:, 3072:3072 + T]
                link(nc.scalar.activation(r, r, ACT.Tanh, scale=0.5, bias=small[:, 8 + c:9 + c]))
                link(nc.scalar.activation(g, g, ACT.Tanh, scale=0.5, bias=small[:, 12 + c:13 + c]))
                ls = small[:, 4 + c:5 + c]
                nc.scalar.activation(la[:, c, :], r, ACT.Exp, scale=ls, bias=ls).then_inc(S_("act_chain"), 1)
                chain.n += 1
                nc.scalar.activation(r, r, ACT.Tanh, scale=ls, bias=ls).then_inc(S_("lru_tanh"), 1)

            def softmax_act(tag):
                units = units_of[tag]
                for n in range(len(units) + 2):
                    if n < len(units):
                        u = units[n]
                        act.wait_ge(*when(tag + "_scored", n + 1))
                        p = Sb[:, n % 4, 0:u["L"]]
                        nc.scalar.activation(p, p, ACT.Exp, scale=-1.0, bias=stat[:, 16 + n % 4:17 + n % 4],
                                             accum_out=stat[:, 20 + n % 4:21 + n % 4]).then_inc(S_(tag + "_exp"), 1)
                        if tag == "swa":
                            nc.scalar.activation(stat[:, 24 + n % 4:25 + n % 4], sinkb[:, u["h"]:u["h"] + 1], ACT.Exp,
                                                 bias=stat[:, 16 + n % 4:17 + n % 4]).then_inc(S_("swa_sink"), 1)
                    m = n - 2
                    if m >= 0:
                        u = units[m]
                        k = len(u["values"])
                        act.wait_ge(*when(tag + "_pt", m + 1))
                        if m >= 2:
                            act.wait_ge(*when(tag + "_pv", m - 1))
                        nc.scalar.activation(PT[:, m % 2, 0:P * k], psum[:, 2048:2048 + P * k], ACT.Copy
                                             ).then_inc(S_(tag + "_pt_copied"), 1)
                    if m >= 8 and (m - 8) % 8 == 0:
                        softmax_out(tag, (m - 8) // 8)
                softmax_out(tag, 3)

            def softmax_out(tag, pair):
                act.wait_ge(*when(tag + "_pv", 8 * pair + 8))
                nc.scalar.activation(QO[:, 1 if tag == "fox" else 0, pair, :], bank(6 + pair % 2), ACT.Copy
                                     ).then_inc(S_(tag + "_out"), 1)

            def norm_squares(tag, src, stored):
                for n in range(KC):
                    if stored == "h_final":
                        act.wait_ge(*when("h_final", n + 1))
                    else:
                        freed(act, (stored, n))
                    if n >= 2:
                        act.wait_ge(*when(tag + "_summed", n - 1))
                    nc.scalar.activation(ntmp[:, n % 2, :], src[:, n, :], ACT.Square).then_inc(S_(tag + "_squared"), 1)

            def root(tag, dst, src):
                act.wait_ge(*when(tag + "_ms", 1))
                nc.scalar.activation(dst, src, ACT.Sqrt).then_inc(S_(tag + "_root"), 1)

            def norm_split(tag, shift):
                o = 52 if tag == "n_one" else 44
                root(tag, stat[:, o:o + 4], stat[:, o - 4:o])
                for n in range(KC):
                    act.wait_ge(*when(tag + "_normed", n + 1))
                    if shift is None:
                        ins = nc.scalar.activation(AH[:, n, :], nout[:, n % 2, :], ACT.Copy)
                    else:
                        ins = nc.scalar.activation(AH[:, n, :], nout[:, n % 2, :], ACT.Identity, bias=shift[:, n:n + 1])
                    ins.then_inc(S_(tag + "_hi"), 1)

            def split_outputs(tag, b, src, dst, needs):
                for sem_name, value in needs:
                    act.wait_ge(*when(sem_name, value))
                nc.scalar.activation(dst, src, ACT.Copy).then_inc(S_(tag + "_oh"), 1)

            def split_merged(tag, src, last_gate):
                act.wait_ge(*when("dense_ready", GROUPS[SLAB_OF[last_gate]["outs"][-1]] + 1))
                for n in range(KC):
                    merged_at(act, tag, (2 if tag == "m1" else 1) * KC + n)
                    nc.scalar.activation(AH[:, n, :], src[:, n, :], ACT.Copy).then_inc(S_(tag + "_hi"), 1)

            def gates_rows():
                g = ("if", 0)
                src = ready(g)
                nc.scalar.activation(ifr[0:8, 0, :], src[0:8, :], ACT.Identity, bias=fbias[0:8, 1:2]
                                     ).then_inc(S_(f"bank_free{BANK[g][0]}"), 1)
                act.wait_ge(*when(f"bank_free{BANK[g][0]}", BANK[g][1] + 1))
                link(nc.scalar.activation(ifr[0:8, 1, :], ifr[0:8, 0, :], ACT.Abs))
                link(nc.scalar.activation(ifr[0:8, 1, :], ifr[0:8, 1, :], ACT.Exp, scale=-1.0))
                nc.scalar.activation(ifr[0:8, 1, :], ifr[0:8, 1, :], ACT.Ln, bias=1.0).then_inc(S_("if_ln"), 1)

            def gates_sums():
                act.wait_ge(*when("if_g", 1))
                link(nc.scalar.activation(ifr[0:4, 4, :], bank(6)[0:4], ACT.Copy))
                nc.scalar.activation(ifr[0:4, 2, :], bank(7)[0:4], ACT.Copy).then_inc(S_("if_g4"), 1)

            def gates_guard():
                act.wait_ge(*when("if_guard", 1))
                link(nc.scalar.activation(ifr[0:4, 6, :], ifr[0:4, 6, :], ACT.Exp))
                act.wait_ge(*when("if_cols", 1))
                nc.scalar.activation(small[:, 80:96], bank(5, 16), ACT.Copy).then_inc(S_("if_ready"), 1)

            def mlstm_act():
                for h in range(C1):
                    for j in range(NB):
                        n = 4 * h + j
                        act.wait_ge(*when("ml_m", h + 1))
                        if n >= 2:
                            act.wait_ge(*when("ml_s", n - 1))
                        gcol = small[:, 80 + 4 * j + h:81 + 4 * j + h]
                        ins = nc.scalar.activation(mE[:, n % 2, 0:P], mMd[:, P * j:P * j + P], ACT.Exp, bias=gcol)
                        if j < NB - 1:
                            ins = nc.scalar.activation(mE[:, n % 2, P:S - P * j], mM[:, P * j + P:], ACT.Exp, bias=gcol)
                        ins.then_inc(S_("ml_e"), 1)
                    act.wait_ge(*when("ml_pv", 4 * h + 4))
                    nc.scalar.activation(rt[:, h % 2, :], bank(4 + h % 2), ACT.Abs).then_inc(S_("ml_absden"), 1)

            def head_squares(tag, src, ready_name):
                for c in range(C1):
                    act.wait_ge(*when(ready_name, c + 1))
                    if c >= 2:
                        act.wait_ge(*when(tag + "_summed", c - 1))
                    nc.scalar.activation(mE[:, c % 2, :], src[:, c, :], ACT.Square).then_inc(S_(tag + "_squared"), 1)

            def diff_act():
                N = 4 * NB
                for n in range(N + 4):
                    if n < N:
                        L = P * (n % NB + 1)
                        act.wait_ge(*when("df_min", n + 1))
                        if n >= 2:
                            act.wait_ge(*when("df_pt", n - 1))
                        for m in range(2):
                            ins = nc.scalar.activation(dP[:, n % 2, m, 0:L], bank(2 * (n % 2) + m, L), ACT.Exp, scale=-1.0,
                                                       bias=small[:, 100 + 2 * (n % 2) + m:101 + 2 * (n % 2) + m],
                                                       accum_out=small[:, 104 + 2 * (n % 2) + m:105 + 2 * (n % 2) + m])
                            ins.then_inc(S_("df_exp"), 1)
                    m = n - 2
                    if 0 <= m < N:
                        act.wait_ge(*when("df_pt", m + 1))
                        if m >= 2:
                            act.wait_ge(*when("df_pv", m - 1))
                        L = P * (m % NB + 1)
                        nc.scalar.activation(dPT[:, m % 2, 0:L], bank(4 + m % 2, L), ACT.Copy).then_inc(S_("df_pt_copied"), 1)
                    m = n - 4
                    if m >= 0 and m % NB == NB - 1:
                        h = m // NB
                        act.wait_ge(*when("df_pv", m + 1))
                        nc.scalar.activation(qkd[:, 0, h, :], bank(6 + h % 2), ACT.Copy).then_inc(S_("df_out"), 1)

            for s in SLABS:
                name = s["name"]
                k = name[0]
                if s["kind"] != "W":
                    continue
                feed(s["h"] + 1)
                if name == ("ffg", 0):
                    norm_split("n_ffn", None)
                if name == ("if", 0):
                    norm_squares("n_fin", hT, "ffo")
                    root("n_fin", stat[:, 44:48], stat[:, 40:44])
                    norm_split("n_one", shift1)
                    act.wait_ge(*when("lam_sums", 2))
                    nc.scalar.activation(small[:, 70:72], bank(6, 2), ACT.Exp).then_inc(S_("lam_exps"), 1)
                if k == "gate" and name[2:] == (0, 0):
                    b = name[1]
                    done = SLAB_OF[("branch", b - 1, 1)]["outs"][-1] if b else ("va", 0, "meta")
                    split_outputs("m1", b, QO[:, b], OH, [("swa_out", 4), ("dense_ready", GROUPS[done] + 1), ("m1_ol", b)] if b
                                  else [("swa_out", 4), ("swa_pv", 32)])
                if k == "gate2" and name[2:] == (0, 0):
                    b = name[1]
                    if b == 0:
                        split_outputs("m2", b, qkm[:, 0], OH2, [("ml_gated", C1), ("df_normed", C1)])
                    else:
                        done = SLAB_OF[("branch2", 0, 1)]["outs"][-1]
                        split_outputs("m2", b, qkd[:, 0], OH2, [("df_normed", C1), ("dense_ready", GROUPS[done] + 1), ("m2_ol", 1)])
                if k == "wo" and name[1] == 0:
                    split_merged("m1", merged, ("gate", 2, 1, 1))
                if k == "wo2" and name[1] == 0:
                    split_merged("m2", merged2, ("gate2", 1, 1, 1))
                for g in s["outs"]:
                    if k in ("vf", "vm", "vd", "branch", "branch2", "wo", "wo2", "ffo", "ffu", "qm", "km") or g[0] == "va":
                        continue
                    if k in ("gate", "gate2"):
                        b, c = g[0][1], g[1]
                        tag = "m1" if k == "gate" else "m2"
                        it = KC * b + c
                        src = ready(g)
                        if it >= 4:
                            merged_at(act, tag, it - 4)
                        if it == 0 and tag == "m2":
                            act.wait_ge(*when("ml_pv", 16))
                        copy_out(g, (gsig if tag == "m1" else gsig2)[:, c % 4, :], src, func=ACT.Sigmoid)
                    elif k == "ffg":
                        c = g[1]
                        src = ready(g)
                        if c >= 2:
                            act.wait_ge(*when("f_lo", c - 1))
                        copy_out(g, ftmp[:, c % 2, :], src, func=ACT.Silu)
                    elif k == "om":
                        copy_out(g, om[:, g[1], :], ready(g), func=ACT.Sigmoid)
                    elif k in ("qd", "kd"):
                        c = g[1] + (C1 if k == "kd" else 0)
                        src = ready(g)
                        link(nc.scalar.activation(qkd[:, c // C1, c % C1, :], src, ACT.Copy))
                        if c >= 3:
                            act.wait_ge(*when("qk_summed", c - 2))
                        nc.scalar.activation(rt[:, c % 3, :], src, ACT.Square).then_inc(S_(f"bank_free{BANK[g][0]}"), 1)
                    elif k == "if":
                        gates_rows()
                    if k == "xc":
                        src = ready(g)
                        dst = xc[:, g[1], 0:M] if len(g) == 3 else xc[:, g[1], M:T]
                        copy_out(g, dst, src[:, 0:M] if len(g) == 3 else src)
                    elif k == "fl":
                        src = ready(g)
                        dst = fl4[0:8, 0, 0:M] if len(g) == 3 else fl4[0:8, 0, M:T]
                        act.wait_ge(*when("params", PARAMS))
                        nc.scalar.activation(dst, src[0:8, 0:M] if len(g) == 3 else src[0:8, :], ACT.Identity,
                                             bias=fbias[0:8, 0:1]).then_inc(S_(f"bank_free{BANK[g][0]}"), 1)
                        if len(g) == 3:
                            act.wait_ge(*when(f"bank_free{BANK[g][0]}", BANK[g][1] + 1))
                            act.wait_ge(*when(f"bank_free{BANK[('fl', 0)][0]}", BANK[("fl", 0)][1] + 1))
                            link(nc.scalar.activation(fl4[0:8, 1, :], fl4[0:8, 0, :], ACT.Abs))
                            link(nc.scalar.activation(fl4[0:8, 1, :], fl4[0:8, 1, :], ACT.Exp, scale=-1.0))
                            nc.scalar.activation(fl4[0:8, 1, :], fl4[0:8, 1, :], ACT.Ln, bias=1.0
                                                 ).then_inc(S_("forget_ln"), 1)
                    elif k == "yc":
                        copy_out(g, QO[:, 2, g[1], :], ready(g), func=ACT.Gelu_apprx_tanh)
                    elif k == "kf":
                        src = ready(g)
                        if len(g) == 3:
                            copy_out(g, kf[:, g[1], 0:M], src[:, 0:M])
                        else:
                            copy_out(g, kf[:, g[1], M:T], src)
                    elif k == "kava":
                        src = ready(g)
                        if len(g) == 3:
                            copy_out(g, ka[:, 0:M], src[:, 0:M])
                        else:
                            copy_out(g, ka[:, M:T], src)
                    elif k == "qf":
                        act.wait_ge(*when("skew_written", 16))
                        copy_out(g, QO[:, 1, g[1], :], ready(g), scale=-DH ** -0.5)
                    elif k == "qa":
                        copy_out(g, QO[:, 0, g[1], :], ready(g), scale=-DH ** -0.5)
                if name in LRU_AFTER:
                    lru_gates(LRU_AFTER.index(name))
                if name == LRU_AFTER[-1]:
                    for c in range(C1):
                        act.wait_ge(*when("lru_ratio", c + 1))
                        nc.scalar.activation(xc[:, c, :], xc[:, c, :], ACT.Sqrt).then_inc(S_("lru_sqrt"), 1)
                if name == ("qf", 1):
                    feed(s["h"] + 2)
                    act.wait_ge(*when("lru_done", C1))
                    for h in range(8):
                        act.wait_ge(*when("cum_rows", h + 1))
                        nc.scalar.activation(cbias[:, h, :], psum[:, 2048 + 1024 * (h % 2):2048 + 1024 * (h % 2) + T], ACT.Copy
                                             ).then_inc(S_("cum_copied"), 1)
                    softmax_act("fox")
                if name == ("kava", 0):
                    feed(s["h"] + 2)
                    softmax_act("swa")
                if k == "ffu":
                    for c in (2 * name[1], 2 * name[1] + 1):
                        freed(act, ("ffu", c))
                        nc.scalar.activation(FH[:, c, :], ftmp[:, c % 2, :], ACT.Copy).then_inc(S_("f_hi"), 1)
                if k in ("wo", "wo2"):
                    tag, sq = ("n_ffn", merged) if k == "wo" else ("n_two", merged2)
                    for c in (2 * name[1], 2 * name[1] + 1):
                        freed(act, (k, c))
                        nc.scalar.activation(sq[:, c, :], hT[:, c, :], ACT.Square).then_inc(S_(tag + "_squared"), 1)
                if k in ("qm", "km"):
                    for c in range(2):
                        freed(act, (k, 2 * name[1] + c))
                        c = 2 * name[1] + c + (C1 if k == "km" else 0)
                        x = qkm[:, c // C1, c % C1, :]
                        nc.scalar.activation(x, x, ACT.Silu).then_inc(S_("mconv_silu"), 1)
                if name == ("qm", 0):
                    gates_sums()
                if name == ("qm", 1):
                    gates_guard()
                if name == ("km", 0):
                    act.wait_ge(*when("angles", 1))
                    nc.scalar.activation(sin, ang[:, 0, :], ACT.Sin).then_inc(S_("sincos"), 1)
                    nc.scalar.activation(cos, ang[:, 1, :], ACT.Sin).then_inc(S_("sincos"), 1)
                if name == ("vd", 1):
                    feed(s["h"] + 2)
                    root("qk", small[:, 136:200], stat[:, 0:64])
                    mlstm_act()
                    head_squares("mn", qkm[:, 0], "ml_h")
                    root("mn", small[:, 120:136], stat[:, 0:16])
                    diff_act()
                    head_squares("dn", qkd[:, 0], "df_out")
                    root("dn", small[:, 120:136], stat[:, 0:16])
            root("n_two", stat[:, 44:48], stat[:, 40:44])
            act.wait_ge(*when("router_mm", 1))
            nc.scalar.activation(lgT[0:NG + NE, :], bank(6)[0:NG + NE], ACT.Copy).then_inc(S_("logits_copied"), 1)
            act.wait_ge(*when("group_gap", 1))
            nc.scalar.activation(ge, gd, ACT.Exp).then_inc(S_("group_exp"), 1)
            for t in range(NB):
                act.wait_ge(*when("token_major", 2 * t + 1))
                nc.scalar.activation(h2t[:, t, 0:512], bank(2 * t % 4), ACT.Copy).then_inc(S_("h2t_even"), 1)
            act.wait_ge(*when("choice_gap", 1))
            nc.scalar.activation(choice_exp, choice_gap, ACT.Exp).then_inc(S_("choice_exp"), 1)
            for t in range(NB):
                act.wait_ge(*when("token_major", 2 * NB + 2 * t + 1))
                nc.scalar.activation(xtm[:, t, 0:512], bank(2 * t % 4), ACT.Copy).then_inc(S_("xtm_even"), 1)
            act.wait_ge(*when("g2_mm", 1))
            nc.scalar.activation(g2row[:, 0:512], bank(4), ACT.Copy).then_inc(S_("g2_even"), 1)

            def xt_copy(i, u):
                n = UN * i + u
                if not (isinstance(i, int) and i == 0):
                    act.wait_ge(*when("gu_done", n - (UN - 1)))
                act.wait_ge(*when("tx_done", n + 1))
                nc.scalar.activation(XT[:, u, 0:512], bank(0), ACT.Copy).then_inc(S_("xt_even"), 1)

            def tile_out(i, u):
                n = UN * i + u
                act.wait_ge(*when("ta_done", n + 1))
                if not (isinstance(i, int) and i == 0):
                    act.wait_ge(*when("y_done", n - (UN - 1)))
                nc.scalar.activation(AT[:, u, :], bank(2, 2 * P), ACT.Copy).then_inc(S_("at_ready"), 1)

            def y_copy(i, u):
                n = UN * i + u
                if not (isinstance(i, int) and i == 0):
                    act.wait_ge(*when(f"y_stored{u}", 16 * i))
                act.wait_ge(*when("y_done", n + 1))
                nc.scalar.activation(Yt[:, u, 0:512], bank(4), ACT.Copy).then_inc(S_("y_even"), 1)

            def silu(i, u):
                n = UN * i + u
                act.wait_ge(*when("gu_done", n + 1))
                if not (isinstance(i, int) and i == 0):
                    act.wait_ge(*when("act_ready", n - (UN - 1)))
                nc.scalar.activation(sA[:, u, :], bank(3, DE), ACT.Silu).then_inc(S_("silu_ready"), 1)

            def step(i, u, ahead, before):
                if ahead:
                    xt_copy(*ahead)
                if before:
                    tile_out(*before)
                silu(i, u)
                if before:
                    y_copy(*before)

            xt_copy(0, 0)
            run_tiles(act, step)
            tile_out(TURNS - 1, UN - 1)
            y_copy(TURNS - 1, UN - 1)
            with act.If(more_tiles(act)):
                xt_copy(TURNS, 0)
                run_overflow(step)
                tile_out(NT // UN - 1, UN - 1)
                y_copy(NT // UN - 1, UN - 1)
            for t in range(NB):
                act.wait_ge(*when(f"yg_landed{t}", 32))
                act.wait_ge(*when("choice_weights", 1))
                nc.scalar.activation(yg[:, 0, t, :], yg[:, 0, t, :], ACT.Copy, scale=weight1[:, t:t + 1]
                                     ).then_inc(S_("y1_scaled"), 1)

        @block.vector
        def _(dve):
            V = nc.vector
            chain = Count(S_("dve_chain"))

            def link(ins):
                chain(ins)
                dve.wait_ge(chain.sem, chain.n)

            fed = [0]

            def feed(h):
                while fed[0] <= min(h, last_h):
                    s = W_SLABS[fed[0]]
                    dve.wait_ge(*when("hi_ready", fed[0] + 1))
                    w, n = width(s), fed[0] % HL
                    V.tensor_tensor(WL[:, n, 0:w], raw[:, s["n"] % RAW, 0:w], WH[:, n, 0:w].bitcast(F32), ALU.subtract
                                    ).then_inc(S_("lo_ready"), 1)
                    fed[0] += 1

            def ready(g):
                dve.wait_ge(*when("dense_ready", GROUPS[g] + 1))
                return bank(BANK[g][0])

            dve.wait_ge(*when("rms1", 2))
            link(V.reciprocal(stat[:, 32:36], stat[:, 8:12]))
            link(V.reciprocal(stat[0:M, 36:37], stat[0:M, 12:13]))
            for t in range(NB):
                V.tensor_scalar(xs[:, t, :], xin[:, t, :], stat[:, 32 + t:33 + t], None, ALU.mult).then_inc(S_("xs_ready"), 1)
            V.tensor_scalar(xms[0:M, :], xm[0:M, :], stat[0:M, 36:37], None, ALU.mult).then_inc(S_("xs_ready"), 1)
            na, nb = sum(n for _, n in ROWS_A), sum(n for _, n in ROWS_B)
            dve.wait_ge(*when("col_mm", 1))
            V.tensor_copy(pcol[:, 0:na], bank(7, na)).then_inc(S_("cols"), 1)
            dve.wait_ge(*when("cols", 1))

            def un_lo(u):
                t, half = u // 2, u % 2
                dve.wait_ge(*when("uh_ready", u + 1))
                V.tensor_tensor(AL[:, 4 * half:4 * half + 4, P * t:P * t + P], utmp[:, u % 2, :].rearrange("p (k n) -> p k n", k=4),
                                AH[:, 4 * half:4 * half + 4, P * t:P * t + P].bitcast(F32), ALU.subtract
                                ).then_inc(S_("ul_ready"), 1)

            for u in range(2 * NB):
                half = u % 2
                dve.wait_ge(*when("us_ready", u + 1))
                if u >= 2:
                    dve.wait_ge(*when("uh_ready", u - 1))
                    dve.wait_ge(*when("ul_ready", u - 1))
                V.tensor_tensor(utmp[:, u % 2, :].rearrange("p (k n) -> p k n", k=4), bank(6 + u % 2).rearrange("p (k n) -> p k n", k=4),
                                col("norm_mix", 4 * half, 4).unsqueeze(2).to_broadcast([P, 4, P]), ALU.mult
                                ).then_inc(S_("un_ready"), 1)
                if u:
                    un_lo(u - 1)
            un_lo(2 * NB - 1)
            feed(1)
            dve.wait_ge(*when("um_mm", 1))
            dve.wait_ge(*when("ul_ready", 8))
            um = utmp[:, 0, 0:KC * M].rearrange("p (k n) -> p k n", k=KC)
            dve.wait_ge(*when("pool_set", 3))
            V.tensor_tensor(um, bank(4, KC * M).rearrange("p (k n) -> p k n", k=KC),
                            col("norm_mix", 0, 8).unsqueeze(2).to_broadcast([P, KC, M]), ALU.mult).then_inc(S_("um_ready"), 1)
            dve.wait_ge(*when("umh_ready", 1))
            V.tensor_tensor(AML[:, :, 0:M], um, AMH[:, :, 0:M].bitcast(F32), ALU.subtract).then_inc(S_("uml_ready"), 1)

            lam, z, z2, pl = col("lru_lambda", 0, 4), small[:, 16:20], small[:, 20:24], small[:, 24:28]
            link(V.tensor_scalar(small[:, 28:32], lam, -1.0, None, ALU.mult))
            V.tensor_tensor(small[:, 32:36], lam, small[:, 28:32], ALU.max).then_inc(S_("lam_abs"), 1)
            dve.wait_ge(*when("lam_exp", 1))
            link(V.tensor_scalar(z2, small[:, 36:40], 2.0, None, ALU.add))
            link(V.reciprocal(z2, z2))
            link(V.tensor_tensor(z, small[:, 36:40], z2, ALU.mult))
            link(V.tensor_tensor(z2, z, z, ALU.mult))
            link(V.tensor_scalar(pl, z2, 1.0 / 17, 1.0 / 15, ALU.mult, ALU.add))
            for n in (13, 11, 9, 7, 5, 3, 1):
                link(V.tensor_tensor(pl, pl, z2, ALU.mult))
                link(V.tensor_scalar(pl, pl, 1.0 / n, None, ALU.add))
            link(V.tensor_tensor(pl, pl, z, ALU.mult))
            link(V.tensor_scalar(z, lam, 0.0, 4.0, ALU.min, ALU.mult))
            link(V.scalar_tensor_tensor(small[:, 4:8], pl, -8.0, z, ALU.mult, ALU.add))
            link(V.tensor_scalar(small[:, 8:12], col("lru_b_r", 0, 4), 0.5, None, ALU.mult))
            V.tensor_scalar(small[:, 12:16], col("lru_b_i", 0, 4), 0.5, None, ALU.mult).then_inc(S_("lru_cols"), 1)

            def distance_rows():
                dve.wait_ge(*when("col_b_mm", 1))
                V.tensor_copy(pcol[:, P:P + nb], bank(5, nb)).then_inc(S_("cols_b"), 1)
                for h in range(8):
                    dve.wait_ge(*when("dist_mm", h + 1))
                    V.scalar_tensor_tensor(stage[:, h, :], bank(6 + h % 2, SKEW), -1.0, K("dist_mask"), ALU.mult, ALU.add
                                           ).then_inc(S_("stage_ready"), 1)

            def lru_conv(c):
                for g in (("xc", c), ("xc", c, "meta")):
                    dve.wait_ge(*when(f"bank_free{BANK[g][0]}", BANK[g][1] + 1))
                link(V.tensor_scalar(cv[:, c, :], xc[:, c, :], col("conv_w", 12 + c), col("conv_b", c), ALU.mult, ALU.add))
                for i in (2, 1, 0):
                    o = 3 - i
                    ins = V.scalar_tensor_tensor(cv[:, c, o:], xc[:, c, 0:T - o], col("conv_w", 4 * i + c), cv[:, c, o:],
                                                 ALU.mult, ALU.add)
                    if i:
                        link(ins)
                    else:
                        ins.then_inc(S_("conv_ready"), 1)

            def lru_mix(c):
                r, g = psum[:, 2048:2048 + T], psum[:, 3072:3072 + T]
                dve.wait_ge(*when("lru_tanh", c + 1))
                link(V.tensor_scalar(xc[:, c, :], r, -1.0, 1.0, ALU.mult, ALU.add))
                link(V.reciprocal(xc[:, c, :], xc[:, c, :]))
                V.scalar_tensor_tensor(xc[:, c, :], r, -0.5, xc[:, c, :], ALU.mult, ALU.mult).then_inc(S_("lru_ratio"), 1)
                V.scalar_tensor_tensor(cv[:, c, :], g, 1.0, cv[:, c, :], ALU.add, ALU.mult).then_inc(S_("lru_psum_read"), 1)

            def lru_scan(c):
                dve.wait_ge(*when("lru_sqrt", c + 1))
                dve.wait_ge(*when("lru_psum_read", c + 1))
                link(V.tensor_tensor(cv[:, c, :], cv[:, c, :], xc[:, c, :], ALU.mult))
                link(V.tensor_tensor_scan(la[:, c, :], la[:, c, :], cv[:, c, :], 0.0, ALU.mult, ALU.add))
                g = ("yc", c)
                dve.wait_ge(*when(f"bank_free{BANK[g][0]}", BANK[g][1] + 1))
                V.tensor_tensor(QO[:, 2, c, :], QO[:, 2, c, :], la[:, c, M:T], ALU.mult).then_inc(S_("lru_done"), 1)

            def inverse(tag, x):
                dve.wait_ge(*when(tag + "_root", 1))
                V.reciprocal(x, x).then_inc(S_(tag + "_rms"), 1)

            def norm_apply(tag, src, gcols, split, out_name=None, shift=None, dst=None):
                dve.wait_ge(*when(tag + "_summed", KC))
                V.tensor_scalar(stat[:, 40:44], bank(4, 4), 1.0 / D, EPS, ALU.mult, ALU.add).then_inc(S_(tag + "_ms"), 1)
                inverse(tag, stat[:, 44:48])
                dve.wait_ge(*when(tag + "_bc", 1))
                for n in range(KC):
                    if split:
                        if n >= 2:
                            dve.wait_ge(*when(tag + "_lo", n - 1))
                        V.scalar_tensor_tensor(nout[:, n % 2, :], src[:, n, :], gcols[:, n:n + 1], bank(5), ALU.mult, ALU.mult
                                               ).then_inc(S_(tag + "_normed"), 1)
                        m = n - 1
                        if m >= 0:
                            norm_lo(tag, m, shift)
                    elif shift is not None:
                        link(V.scalar_tensor_tensor(dst[:, n, :], src[:, n, :], gcols[:, n:n + 1], bank(5), ALU.mult, ALU.mult))
                        V.tensor_scalar(dst[:, n, :], dst[:, n, :], shift[:, n:n + 1], None, ALU.add).then_inc(S_(out_name), 1)
                    else:
                        V.scalar_tensor_tensor(dst[:, n, :], src[:, n, :], gcols[:, n:n + 1], bank(5), ALU.mult, ALU.mult
                                               ).then_inc(S_(out_name), 1)
                if split:
                    norm_lo(tag, KC - 1, shift)

            def two_norms():
                r1, ms2, r2, r12, wg = stat[:, 44:48], stat[:, 48:52], stat[:, 52:56], stat[:, 56:60], small[:, 200:208]
                w = col("norm_final", 0, 8)
                link(V.tensor_tensor(wg, w, gain, ALU.mult))
                dve.wait_ge(*when("n_fin_summed", KC))
                V.tensor_scalar(stat[:, 40:44], bank(4, 8)[:, 0:8:2], 1.0 / D, EPS, ALU.mult, ALU.add).then_inc(S_("n_fin_ms"), 1)
                inverse("n_fin", r1)
                dve.wait_ge(*when("n_fin_rms", 1))
                link(V.tensor_tensor(ms2, bank(4, 8)[:, 1:8:2], r1, ALU.mult))
                link(V.tensor_tensor(ms2, ms2, r1, ALU.mult))
                V.tensor_scalar(ms2, ms2, 1.0 / D, EPS, ALU.mult, ALU.add).then_inc(S_("n_one_ms"), 1)
                dve.wait_ge(*when("n_one_root", 1))
                link(V.reciprocal(r2, r2))
                V.tensor_tensor(r12, r2, r1, ALU.mult).then_inc(S_("n_one_rms"), 1)
                dve.wait_ge(*when("n_one_bc", 1))
                for n in range(KC):
                    if n >= 2:
                        dve.wait_ge(*when("n_one_lo", n - 1))
                    V.scalar_tensor_tensor(nout[:, n % 2, :], hT[:, n, :], wg[:, n:n + 1], bank(7), ALU.mult, ALU.mult
                                           ).then_inc(S_("n_one_normed"), 1)
                    if n:
                        norm_lo("n_one", n - 1, shift1)
                norm_lo("n_one", KC - 1, shift1)
                for n in range(KC):
                    V.scalar_tensor_tensor(hT[:, n, :], hT[:, n, :], w[:, n:n + 1], bank(5), ALU.mult, ALU.mult
                                           ).then_inc(S_("h_final"), 1)

            def norm_lo(tag, n, shift):
                dve.wait_ge(*when(tag + "_hi", n + 1))
                hi = AH[:, n, :].bitcast(F32)
                if shift is None:
                    ins = V.tensor_tensor(AL[:, n, :], nout[:, n % 2, :], hi, ALU.subtract)
                else:
                    ins = V.scalar_tensor_tensor(AL[:, n, :], nout[:, n % 2, :], shift[:, n:n + 1], hi, ALU.add, ALU.subtract)
                ins.then_inc(S_(tag + "_lo"), 1)

            def gates_rows():
                dve.wait_ge(*when("if_ln", 1))
                f8 = slice(0, 8)
                link(V.tensor_scalar(ifr[f8, 2, :], ifr[f8, 0, :], 0.0, None, ALU.min))
                link(V.tensor_tensor(ifr[f8, 1, :], ifr[f8, 1, :], ifr[f8, 2, :], ALU.subtract))
                link(V.memset(ifr[f8, 2, :], 1.0))
                V.tensor_tensor_scan(ifr[f8, 3, :], ifr[f8, 2, :], ifr[f8, 1, :], 0.0, ALU.mult, ALU.add
                                     ).then_inc(S_("if_cum"), 1)

            def gates_maximum():
                dve.wait_ge(*when("if_g4", 1))
                link(V.tensor_tensor_scan(ifr[0:4, 5, :], ifr[0:4, 4, :], ifr[0:4, 4, :], 0.0, ALU.max, ALU.max))
                V.tensor_tensor(ifr[0:4, 6, :], ifr[0:4, 2, :], ifr[0:4, 5, :], ALU.subtract).then_inc(S_("if_guard"), 1)
                V.tensor_scalar(ifr[0:4, 5, :], ifr[0:4, 5, :], -1.0, None, ALU.mult).then_inc(S_("if_negm"), 1)

            def conv4(g, c):
                src = ready(g)
                x = qkm[:, c // C1, c % C1, :]
                link(V.tensor_scalar(x, src, col("conv_w_2", 24 + c), col("conv_b_2", c), ALU.mult, ALU.add))
                for i in (2, 1, 0):
                    o = 3 - i
                    ins = V.scalar_tensor_tensor(x[:, o:], src[:, 0:S - o], col("conv_w_2", 8 * i + c), x[:, o:], ALU.mult, ALU.add)
                    if i:
                        link(ins)
                ins.then_inc(S_(f"bank_free{BANK[g][0]}"), 1)

            def mlstm_dve():
                dve.wait_ge(*when("pool_set", 9))

                def running_max(h):
                    dve.wait_ge(*when("ml_bc", h + 1))
                    if h:
                        dve.wait_ge(*when("ml_e", 4 * h))
                    V.tensor_copy(mM, bank(6)).then_inc(S_("dve_chain"), 1)
                    chain.n += 1
                    V.tensor_tensor(mMd.rearrange("p (j n) -> p j n", j=NB), bank(6).rearrange("p (j n) -> p j n", j=NB),
                                    maskT.unsqueeze(1).to_broadcast([P, NB, P]), ALU.add).then_inc(S_("ml_m"), 1)

                def head_out(h):
                    dve.wait_ge(*when("ml_absden", h + 1))
                    den = rt[:, h % 2, :]
                    link(V.tensor_tensor(den, den, bank(7), ALU.max))
                    link(V.reciprocal(den, den))
                    V.tensor_tensor(qkm[:, 0, h, :], bank(2 + h % 2), den, ALU.mult).then_inc(S_("ml_h"), 1)

                running_max(0)
                for h in range(C1):
                    for j in range(NB):
                        n, N = 4 * h + j, S - P * j
                        dve.wait_ge(*when("ml_e", n + 1))
                        dve.wait_ge(*when("ml_qk", n + 1))
                        if n >= 2:
                            dve.wait_ge(*when("ml_pv", n - 1))
                        V.scalar_tensor_tensor(mS[:, n % 2, 0:N], bank(n % 2, N), P ** -0.5, mE[:, n % 2, 0:N], ALU.mult, ALU.mult
                                               ).then_inc(S_("ml_s"), 1)
                        if j == 0 and h:
                            head_out(h - 1)
                    if h < C1 - 1:
                        running_max(h + 1)
                head_out(C1 - 1)

            def head_norm(tag, src, wcol, out_name, post=None):
                dve.wait_ge(*when(tag + "_summed", C1))
                V.tensor_scalar(stat[:, 0:16], bank(4, 16), 1.0 / P, EPS, ALU.mult, ALU.add).then_inc(S_(tag + "_ms"), 1)
                inverse(tag, small[:, 120:136])
                for c in range(C1):
                    dve.wait_ge(*when(tag + "_bc", c + 1))
                    ins = V.scalar_tensor_tensor(src[:, c, :], src[:, c, :], wcol(c), bank(6 + c % 2), ALU.mult, ALU.mult)
                    if post is not None:
                        ins.then_inc(S_(tag + "_applied"), 1)
                        dve.wait_ge(*when(tag + "_applied", c + 1))
                        ins = V.tensor_tensor(src[:, c, :], src[:, c, :], post[:, c, :], ALU.mult)
                    ins.then_inc(S_(out_name), 1)

            def rope_dve():
                dve.wait_ge(*when("qk_summed", 8))
                V.tensor_scalar(stat[:, 0:64], bank(4, 64), 1.0 / DH, EPS, ALU.mult, ALU.add).then_inc(S_("qk_ms"), 1)
                inverse("qk", small[:, 136:200])
                link(V.tensor_scalar(small[:, 96:97], col("q_norm_w_2"), -DH ** -0.5, None, ALU.mult))
                dve.wait_ge(*when("sincos", 2))
                def normed(c):
                    x = qkd[:, c // C1, c % C1, :]
                    dve.wait_ge(*when("qk_bc", c + 1))
                    V.scalar_tensor_tensor(x, x, small[:, 96:97] if c < C1 else col("k_norm_w_2"), bank(5 + 2 * (c % 2)), ALU.mult,
                                           ALU.mult).then_inc(S_("qk_normed"), 1)

                normed(0)
                for c in range(8):
                    x, t = qkd[:, c // C1, c % C1, :], rt[:, c % 2, :]
                    if c < 7:
                        normed(c + 1)
                    dve.wait_ge(*when("qk_swap", c + 1))
                    V.tensor_tensor(t, bank(6 - 2 * (c % 2)), sin, ALU.mult).then_inc(S_("qk_swapped"), 1)
                    link(V.tensor_tensor(x, x, cos, ALU.mult))
                    V.tensor_tensor(x, x, t, ALU.add).then_inc(S_("qk_roped"), 1)
                dve.wait_ge(*when("qk_roped", 8))

            def diff_dve():
                for n in range(4 * NB + 1):
                    if n < 4 * NB:
                        L = P * (n % NB + 1)
                        dve.wait_ge(*when("df_qk", n + 1))
                        if n >= 2:
                            dve.wait_ge(*when("df_exp", 2 * n - 2))
                        for m in range(2):
                            k_ = 100 + 2 * (n % 2) + m
                            ins = V.tensor_reduce(small[:, k_:k_ + 1], bank(2 * (n % 2) + m, L), AX_X, ALU.min)
                        ins.then_inc(S_("df_min"), 1)
                    m = n - 1
                    if m >= 0:
                        L, o = P * (m % NB + 1), 2 * (m % 2)
                        dve.wait_ge(*when("df_exp", 2 * m + 2))
                        inv = small[:, 108 + o:110 + o]
                        link(V.reciprocal(inv, small[:, 104 + o:106 + o]))
                        link(V.tensor_tensor(small[:, 109 + o:110 + o], small[:, 109 + o:110 + o], nlam, ALU.mult))
                        p0, p1 = dP[:, m % 2, 0, 0:L], dP[:, m % 2, 1, 0:L]
                        link(V.tensor_scalar(p0, p0, small[:, 108 + o:109 + o], None, ALU.mult))
                        V.scalar_tensor_tensor(p0, p1, small[:, 109 + o:110 + o], p0, ALU.mult, ALU.add).then_inc(S_("df_p"), 1)

            def angles():
                dve.wait_ge(*when("pos_landed", 16))
                link(V.tensor_copy(ang[:, 2, :], posi))
                link(V.tensor_scalar(ang[:, 2, :], ang[:, 2, :], K("inv_freq"), None, ALU.mult))
                two_pi = 2 * np.pi
                c1 = 6.28125
                c2 = float(np.float32(np.round((two_pi - c1) * 2 ** 20) / 2 ** 20))
                c3 = float(np.float32(two_pi - c1 - c2))
                magic = 12582912.0
                for i, quarter in ((0, 0.0), (1, 0.25)):
                    turns = ang[:, 3, :]
                    x = ang[:, i, :]
                    link(V.tensor_scalar(turns, ang[:, 2, :], 1.0 / two_pi, quarter, ALU.mult, ALU.add))
                    link(V.tensor_scalar(turns, turns, magic, None, ALU.add))
                    link(V.tensor_scalar(turns, turns, magic, None, ALU.subtract))
                    src = ang[:, 2, :]
                    for cc in (c1, c2, c3):
                        link(V.scalar_tensor_tensor(x, turns, -cc, src, ALU.mult, ALU.add))
                        src = x
                    if quarter:
                        link(V.tensor_scalar(x, x, np.pi / 2, None, ALU.add))
                    lim = 3.1415925
                    ins = V.tensor_scalar(x, x, lim, -lim, ALU.min, ALU.max)
                    if i == 0:
                        link(ins)
                    else:
                        ins.then_inc(S_("angles"), 1)

            def softmax_dve(tag):
                units = units_of[tag]
                for n in range(len(units) + 1):
                    if n < len(units):
                        u = units[n]
                        dve.wait_ge(*when(tag + "_qk", n + 1))
                        if n >= 4:
                            dve.wait_ge(*when(tag + "_pt", n - 3))
                        start = 3e38
                        if tag == "swa":
                            start = sinkb[:, 8 + u["h"]:9 + u["h"]]
                        V.tensor_tensor_reduce(Sb[:, n % 4, 0:u["L"]], psum[:, 1024 * (n % 2):1024 * (n % 2) + u["L"]],
                                               u["bias"], 1.0, start, ALU.add, ALU.min,
                                               stat[:, 16 + n % 4:17 + n % 4]).then_inc(S_(tag + "_scored"), 1)
                    m = n - 1
                    if m >= 0:
                        L = units[m]["L"]
                        den, inv = stat[:, 20 + m % 4:21 + m % 4], stat[:, 28 + m % 4:29 + m % 4]
                        dve.wait_ge(*when(tag + "_exp", m + 1))
                        if tag == "swa":
                            dve.wait_ge(*when("swa_sink", m + 1))
                            link(V.tensor_tensor(den, den, stat[:, 24 + m % 4:25 + m % 4], ALU.add))
                        link(V.reciprocal(inv, den))
                        V.tensor_scalar(Sb[:, m % 4, 0:L], Sb[:, m % 4, 0:L], inv, None, ALU.mult).then_inc(S_(tag + "_p"), 1)

            def ada_sums(s):
                sem, value = landed[s["n"]]
                dve.wait_ge(*when(f"raw_landed{sem}", value))
                i = s["a"]
                if i == 0:
                    dve.wait_ge(*when("spare_written", 16))
                if i >= 2:
                    dve.wait_ge(*when("ada_used", i - 1))
                w, acc = raw[:, s["n"] % RAW, :].rearrange("p (k n) -> p k n", k=KC), ada_acc[i % 2]
                link(V.tensor_scalar(acc, w[:, 0, :], col("c_2"), None, ALU.mult))
                for c in range(1, KC):
                    ins = V.scalar_tensor_tensor(acc, w[:, c, :], col("c_2", c), acc, ALU.mult, ALU.add)
                    if c < KC - 1:
                        link(ins)
                ins.then_inc(S_("ada_summed"), 1)

            summed = []

            def modulation():
                dve.wait_ge(*when("ada_used", 24))
                V.tensor_tensor(mod, bank(6, 48), col("b_ada_2", 0, 48), ALU.add).then_inc(S_("mod_ready"), 1)
                dve.wait_ge(*when("mod_ready", 1))
                link(V.scalar_tensor_tensor(gain, scale1, 1.0, col("norm1_w_2", 0, 8), ALU.add, ALU.mult))
                link(V.tensor_tensor(wsq[:, :, 1], col("norm_final", 0, 8), col("norm_final", 0, 8), ALU.mult))
                link(V.memset(wsq[:, :, 0], 1.0))
                V.tensor_tensor(small[0:DH, 68:70], small[0:DH, 64:68:2], small[0:DH, 65:68:2], ALU.mult).then_inc(S_("lam_prod"), 1)
                V.tensor_scalar(small[:, 112:116], col("subln_w_2").to_broadcast([P, 4]), 0.8, None, ALU.mult
                                ).then_inc(S_("lam_prod"), 1)

            nlam = small[:, 97:98]
            for s in SLABS:
                name = s["name"]
                k = name[0]
                if s["kind"] == "A":
                    if s["a"] not in summed:
                        ada_sums(s)
                    continue
                after = SLABS[s["n"] + 1:s["n"] + 2]
                if after and after[0]["kind"] == "A":
                    summed.append(after[0]["a"])
                    ada_sums(after[0])
                feed(s["h"] + 1)
                if name == ("ffg", 0):
                    norm_apply("n_ffn", hT, col("norm_ffn", 0, 8), True)
                if name == ("ffo", 0):
                    modulation()
                if name == ("if", 0):
                    two_norms()
                    link(V.scalar_tensor_tensor(gain, scale2, 1.0, col("norm2_w_2", 0, 8), ALU.add, ALU.mult))
                    dve.wait_ge(*when("lam_exps", 1))
                    link(V.tensor_tensor(nlam, small[:, 71:72], small[:, 70:71], ALU.subtract))
                    link(V.tensor_scalar(nlam, nlam, -0.2, None, ALU.add))
                if k in ("gate", "gate2") and name[2:] == (0, 0):
                    tag, b = ("m1" if k == "gate" else "m2"), name[1]
                    src = QO[:, b] if tag == "m1" else (qkm if b == 0 else qkd)[:, 0]
                    hi, lo = (OH, OL) if tag == "m1" else (OH2, OL2)
                    dve.wait_ge(*when(tag + "_oh", b + 1))
                    V.tensor_tensor(lo, src, hi.bitcast(F32), ALU.subtract).then_inc(S_(tag + "_ol"), 1)
                if k in ("wo", "wo2") and name[1] == 0:
                    tag, mg = ("m1", merged) if k == "wo" else ("m2", merged2)
                    for n in range(KC):
                        dve.wait_ge(*when(tag + "_hi", n + 1))
                        V.tensor_tensor(AL[:, n, :], mg[:, n, :], AH[:, n, :].bitcast(F32), ALU.subtract
                                        ).then_inc(S_(tag + "_lo"), 1)
                for g in s["outs"]:
                    if k in ("branch", "branch2"):
                        b, c = g[0][1], g[1]
                        tag = "m1" if k == "branch" else "m2"
                        gs, mg = (gsig, merged) if tag == "m1" else (gsig2, merged2)
                        src = ready(g)
                        gate = ("gate" if tag == "m1" else "gate2", b)
                        dve.wait_ge(*when(f"bank_free{BANK[(gate, c)][0]}", BANK[(gate, c)][1] + 1))
                        if b == 0:
                            V.tensor_tensor(mg[:, c, :], gs[:, c % 4, :], src, ALU.mult).then_inc(S_(f"bank_free{BANK[g][0]}"), 1)
                        else:
                            V.tensor_tensor(gs[:, c % 4, :], gs[:, c % 4, :], src, ALU.mult).then_inc(S_(f"bank_free{BANK[g][0]}"), 1)
                            freed(dve, g)
                            merged_at(dve, tag, KC * (b - 1) + c)
                            V.tensor_tensor(mg[:, c, :], mg[:, c, :], gs[:, c % 4, :], ALU.add).then_inc(S_(tag + "_merged"), 1)
                    elif k in ("wo", "wo2", "ffo"):
                        src = ready(g)
                        n = g[1]
                        if k == "wo2":
                            ins = V.scalar_tensor_tensor(hT[:, n, :], src, gate1[:, n:n + 1], hT[:, n, :], ALU.mult, ALU.add)
                        else:
                            ins = V.tensor_tensor(hT[:, n, :], src, hT[:, n, :], ALU.add)
                        ins.then_inc(S_(f"bank_free{BANK[g][0]}"), 1)
                    elif k == "ffu":
                        c = g[1]
                        src = ready(g)
                        gg = ("ffg", c)
                        dve.wait_ge(*when(f"bank_free{BANK[gg][0]}", BANK[gg][1] + 1))
                        V.tensor_tensor(ftmp[:, c % 2, :], ftmp[:, c % 2, :], src, ALU.mult).then_inc(S_(f"bank_free{BANK[g][0]}"), 1)
                    elif k in ("qm", "km"):
                        conv4(g, g[1] + (C1 if k == "km" else 0))
                    elif k in ("vm", "vd"):
                        src = ready(g)
                        (V.tensor_copy((vm if k == "vm" else vd)[:, g[2], 256 * g[1]:256 * g[1] + 256], src[:, 0:256])
                         ).then_inc(S_(f"bank_free{BANK[g][0]}"), 1)
                    if k == "vf":
                        src = ready(g)
                        if g[2] == "meta":
                            ins = V.tensor_copy(vfm[0:M, 256 * g[1]:256 * g[1] + 256], src[0:M, 0:256])
                        else:
                            ins = V.tensor_copy(vf[:, g[2], 256 * g[1]:256 * g[1] + 256], src[:, 0:256])
                        ins.then_inc(S_(f"bank_free{BANK[g][0]}"), 1)
                    elif g[0] == "va":
                        src = ready(g)
                        if g[2] == "meta":
                            ins = V.tensor_copy(vam[0:M, :], src[0:M, 0:P])
                        else:
                            ins = V.tensor_copy(va[:, g[2], :], src[:, 0:P])
                        ins.then_inc(S_(f"bank_free{BANK[g][0]}"), 1)
                if name == ("xc", 0):
                    distance_rows()
                if name == ("yc", 0):
                    for c in range(C1):
                        lru_conv(c)
                    dve.wait_ge(*when("forget_ln", 1))
                    link(V.tensor_scalar(fl4[0:8, 0, :], fl4[0:8, 0, :], 0.0, None, ALU.min))
                    link(V.tensor_tensor(fl4[0:8, 1, :], fl4[0:8, 0, :], fl4[0:8, 1, :], ALU.subtract))
                    link(V.memset(fl4[0:8, 0, :], 1.0))
                    V.tensor_tensor_scan(fl4[0:8, 2, :], fl4[0:8, 0, :], fl4[0:8, 1, :], 0.0, ALU.mult, ALU.add
                                         ).then_inc(S_("cum_ready"), 1)
                    V.tensor_scalar(sinkb[:, 8:16], sinkb[:, 0:8], -1.0, None, ALU.mult).then_inc(S_("cum_ready"), 1)
                    dve.wait_ge(*when("cum_ready", 2))
                if name in LRU_AFTER:
                    lru_mix(LRU_AFTER.index(name))
                if name == LRU_AFTER[-1]:
                    for c in range(C1):
                        lru_scan(c)
                if name == ("qf", 1):
                    feed(s["h"] + 2)
                    dve.wait_ge(*when("cum_copied", 8))
                    softmax_dve("fox")
                if name == ("kava", 0):
                    feed(s["h"] + 2)
                    dve.wait_ge(*when("sbias_landed", 16 * 8))
                    softmax_dve("swa")
                if k == "ffu":
                    for c in (2 * name[1], 2 * name[1] + 1):
                        dve.wait_ge(*when("f_hi", c + 1))
                        V.tensor_tensor(FL_[:, c, :], ftmp[:, c % 2, :], FH[:, c, :].bitcast(F32), ALU.subtract
                                        ).then_inc(S_("f_lo"), 1)
                if name == ("if", 0):
                    gates_rows()
                if name == ("qm", 0):
                    gates_maximum()
                if name == ("qm", 1):
                    angles()
                if name == ("vd", 1):
                    feed(s["h"] + 2)
                    rope_dve()
                    mlstm_dve()
                    head_norm("mn", qkm[:, 0], lambda c: col("mlstm_norm_w_2", c), "ml_gated", post=om)
                    diff_dve()
                    head_norm("dn", qkd[:, 0], lambda c: small[:, 112:113], "df_normed")
            norm_apply("n_two", hT, gain, False, out_name="h2_ready", shift=shift2, dst=H2)
            V.memset(zero, 0).then_inc(S_("slots_zero"), 1)
            V.tensor_copy(tid, K("token")).then_inc(S_("dve_chain"), 1)
            chain.n += 1
            link(V.tensor_scalar(later, K("expert"), -1000.0, None, ALU.add))
            dve.wait_ge(*when("logits_ready", 1))
            link(V.tensor_tensor(lg, bank(5, NB * (NG + NE)).rearrange("p (t n) -> p t n", t=NB),
                                 rb.unsqueeze(1).to_broadcast([P, NB, NG + NE]), ALU.add))

            def best(x, idx, peak, found, cand):
                w = [P] + list(x.shape[1:])
                link(V.tensor_reduce(peak, x, AX_X, ALU.max))
                link(V.tensor_tensor(cand, x, peak.unsqueeze(2).to_broadcast(w), ALU.is_ge))
                link(V.tensor_tensor(cand, cand, idx.unsqueeze(1).to_broadcast(w), ALU.mult))
                link(V.tensor_reduce(first_, cand, AX_X, ALU.min))
                link(V.tensor_tensor(found, cand, first_.unsqueeze(2).to_broadcast(w), ALU.is_equal))

            first_, gmax, m1_, m2_, pg = (r4[:, n, :] for n in (4, 5, 6, 7, 8))
            gl = lg[:, :, 0:NG]
            best(gl, later[:, 0:NG], gmax, gh, gc)
            V.tensor_tensor(gd, gl, gmax.unsqueeze(2).to_broadcast([P, NB, NG]), ALU.subtract).then_inc(S_("group_gap"), 1)
            shape4 = [P, NB, NG, EPG]
            e4 = em.rearrange("p t (g j) -> p t g j", g=NG)
            gh4 = gh.unsqueeze(3).to_broadcast(shape4)
            link(V.tensor_scalar(gc, gh, -1.0, -LOST, ALU.add, ALU.mult))
            link(V.tensor_tensor(e4, lg[:, :, NG:].rearrange("p t (g j) -> p t g j", g=NG), gh4, ALU.mult))
            link(V.tensor_tensor(e4, e4, gc.unsqueeze(3).to_broadcast(shape4), ALU.add))
            best(em, later, m1_, ohs[:, 0], cnd)
            link(V.scalar_tensor_tensor(em, ohs[:, 0], -3e38, em, ALU.mult, ALU.add))
            best(em, later, m2_, ohs[:, 1], cnd)
            V.tensor_tensor(choice_gap, m2_, m1_, ALU.subtract).then_inc(S_("choice_gap"), 1)
            V.tensor_tensor(both, ohs[:, 0], ohs[:, 1], ALU.add).then_inc(S_("choices"), 1)
            over, incl, base_, cnt = (eN[:, n, :] for n in range(4))
            dve.wait_ge(*when("rank_mm", 1))
            count, rank = bank(7, NE, NB * NE), bank(7, NB * NE).rearrange("p (t n) -> p t n", t=NB)

            def full_tiles(dst, x, extra):
                link(V.tensor_scalar(dst, x, P - extra, None, ALU.is_ge))
                link(V.scalar_tensor_tensor(dst, x, 2 * P - extra, dst, ALU.is_ge, ALU.add))
                link(V.scalar_tensor_tensor(dst, x, 3 * P - extra, dst, ALU.is_ge, ALU.add))

            link(V.tensor_copy(cnt, count))
            full_tiles(over, cnt, -0.5)
            link(V.memset(base_, 1.0))
            link(V.tensor_tensor_scan(incl, base_, over, 0.0, ALU.mult, ALU.add))
            link(V.tensor_tensor(base_, incl, over, ALU.subtract))
            link(V.tensor_scalar(base_, base_, NE - 1.0, None, ALU.add))
            rk, ex, bs, fl_, ov_, sl_ = (r8[:, n] for n in range(6))
            wide = [P, NB, NE]
            for dst, x in ((rk, rank), (ex, K("expert").unsqueeze(1).to_broadcast(wide)), (bs, base_.unsqueeze(1).to_broadcast(wide))):
                link(V.tensor_tensor(prod, ohs, x.unsqueeze(1).to_broadcast([P, 2, NB, NE]), ALU.mult))
                link(V.tensor_reduce(dst, prod, AX_X, ALU.add))
            full_tiles(fl_, rk, 0.5)
            link(V.tensor_scalar(ov_, fl_, 0.5, None, ALU.is_ge))
            link(V.scalar_tensor_tensor(sl_, fl_, -float(P), rk, ALU.mult, ALU.add))
            link(V.tensor_tensor(bs, bs, fl_, ALU.add))
            link(V.tensor_tensor(bs, bs, ex, ALU.subtract))
            link(V.tensor_tensor(bs, bs, ov_, ALU.mult))
            link(V.tensor_tensor(bs, bs, ex, ALU.add))
            link(V.scalar_tensor_tensor(sl_, sl_, float(NT), bs, ALU.mult, ALU.add))
            V.tensor_copy(slotix, sl_).then_inc(S_("slots_ready"), 1)
            link(V.tensor_tensor(ovm, K("expert", NOV).unsqueeze(2).to_broadcast([P, NOV, NE]),
                                 incl.unsqueeze(1).to_broadcast([P, NOV, NE]), ALU.is_ge))
            ends = r8[:, 6].rearrange("p c t -> p (c t)")[:, 0:NOV]
            link(V.tensor_reduce(ends, ovm, AX_X, ALU.add))
            link(V.tensor_scalar(ends, ends, NE - 1.0, None, ALU.min))
            link(V.tensor_copy(eover[:, NOV:NOV + 1], incl[:, NE - 1:NE]))
            V.tensor_copy(eover[:, 0:NOV], ends).then_inc(S_("overflow_ready"), 1)
            for t in range(NB):
                dve.wait_ge(*when("token_major", 2 * t + 2))
                V.tensor_copy(h2t[:, t, 512:], bank((2 * t + 1) % 4)).then_inc(S_("h2t_odd"), 1)
            dve.wait_ge(*when("group_exp", 1))
            dve.wait_ge(*when("choice_exp", 1))
            link(V.tensor_reduce(pg, ge, AX_X, ALU.add))
            link(V.tensor_scalar(weight2, choice_exp, 1.0, None, ALU.add))
            link(V.tensor_tensor(pg, pg, weight2, ALU.mult))
            link(V.reciprocal(weight1, pg))
            V.tensor_tensor(weight2, weight1, choice_exp, ALU.mult).then_inc(S_("choice_weights"), 1)
            for t in range(NB):
                dve.wait_ge(*when("token_major", 2 * NB + 2 * t + 2))
                V.tensor_copy(xtm[:, t, 512:], bank((2 * t + 1) % 4)).then_inc(S_("xtm_odd"), 1)
            dve.wait_ge(*when("g2_mm", 1))
            V.tensor_copy(g2row[:, 512:], bank(5)).then_inc(S_("g2_odd"), 1)

            def pick(i, u):
                n = UN * i + u
                if not (isinstance(i, int) and i == 0):
                    dve.wait_ge(*when(f"xg_landed{u}", 16 * i))
                V.tensor_copy(icol[:, u, :], tok[:, bass.ds(n, 1)]).then_inc(S_("icol_ready"), 1)

            def xt_copy(i, u):
                n = UN * i + u
                if not (isinstance(i, int) and i == 0):
                    dve.wait_ge(*when("gu_done", n - (UN - 1)))
                dve.wait_ge(*when("tx_done", n + 1))
                V.tensor_copy(XT[:, u, 512:], bank(1)).then_inc(S_("xt_odd"), 1)

            def gated(i, u):
                n = UN * i + u
                dve.wait_ge(*when("silu_ready", n + 1))
                V.tensor_tensor(sA[:, u, :], sA[:, u, :], bank(3, DE, DE), ALU.mult).then_inc(S_("act_ready"), 1)

            def y_copy(i, u):
                n = UN * i + u
                if not (isinstance(i, int) and i == 0):
                    dve.wait_ge(*when(f"y_stored{u}", 16 * i))
                dve.wait_ge(*when("y_done", n + 1))
                V.tensor_copy(Yt[:, u, 512:], bank(5)).then_inc(S_("y_odd"), 1)

            def step(i, u, ahead, before):
                if not (isinstance(i, int) and i in (TURNS - 1, NT // UN - 1)):
                    pick(i + 1, u)
                if ahead:
                    xt_copy(*ahead)
                gated(i, u)
                if before:
                    y_copy(*before)

            dve.wait_ge(*when("table_landed", 16))
            for u in range(UN):
                pick(0, u)
            xt_copy(0, 0)
            run_tiles(dve, step)
            y_copy(TURNS - 1, UN - 1)
            with dve.If(more_tiles(dve)):
                for u in range(UN):
                    pick(TURNS, u)
                xt_copy(TURNS, 0)
                run_overflow(step)
                y_copy(NT // UN - 1, UN - 1)
            dve.wait_ge(*when("g2_even", 1))
            dve.wait_ge(*when("g2_odd", 1))
            for t in range(NB):
                y = yg[:, 0, t, :]
                dve.wait_ge(*when("y1_scaled", t + 1))
                link(V.scalar_tensor_tensor(y, yg[:, 1, t, :], weight2[:, t:t + 1], y, ALU.mult, ALU.add))
                link(V.tensor_tensor(y, y, g2row, ALU.mult))
                dve.wait_ge(*when("xtm_even", t + 1))
                V.tensor_tensor(xtm[:, t, :], xtm[:, t, :], y, ALU.add).then_inc(S_("out_ready"), 1)

        @block.tensor
        def _(pe):
            MM = nc.tensor.matmul

            def take(g):
                b, used = BANK[g]
                if used:
                    pe.wait_ge(*when(f"bank_free{b}", used))
                return bank(b)

            def split3(dst, lh, ll, rh, rl, first, last):
                MM(dst, lh, rh, start=first, stop=False)
                MM(dst, lh, rl, start=False, stop=False)
                return MM(dst, ll, rh, start=False, stop=last)

            def slab(s):
                h, name = s["h"], s["name"]
                k = name[0]
                pe.wait_ge(*when("lo_ready", h + 1))
                n = 256
                nk = KC
                if k in ("fl", "if"):
                    n = P
                if k in ("branch", "branch2"):
                    n, nk = 512, C1
                wh = WH[:, h % HL, 0:nk * n].rearrange("p (k n) -> p k n", k=nk)
                wl = WL[:, h % HL, 0:nk * n].rearrange("p (k n) -> p k n", k=nk)
                rh, rl = {"branch": (OH, OL), "branch2": (OH2, OL2)}.get(k, (AH, AL))
                split = {("ffg", 0): "n_ffn_lo", ("if", 0): "n_one_lo", ("wo", 0): "m1_lo", ("wo2", 0): "m2_lo"}.get(name)
                for j, g in enumerate(s["outs"]):
                    dst = take(g)
                    meta = g[-1] == "meta"
                    for c in range(nk):
                        first, last = c == 0, c == nk - 1
                        if split and j == 0:
                            pe.wait_ge(*when(split, c + 1))
                        if g[0] in ("vf", "va", "vm", "vd"):
                            w = slice(P, 2 * P) if g[0] == "va" else slice(0, n)
                            t = 0 if meta else g[2]
                            lh = (AMH if meta else AH)[:, c, P * t:P * t + P]
                            ll = (AML if meta else AL)[:, c, P * t:P * t + P]
                            ins = split3(dst[:, 0:w.stop - w.start], lh, ll, wh[:, c, w], wl[:, c, w], first, last)
                        else:
                            o = (g[1] * P) % n
                            lh, ll = wh[:, c, o:o + P], wl[:, c, o:o + P]
                            if meta:
                                ins = split3(dst[:, 0:M], lh, ll, AMH[:, c, 0:M], AML[:, c, 0:M], first, last)
                            else:
                                ins = split3(dst, lh, ll, rh[:, c, :], rl[:, c, :], first, last)
                    ins.then_inc(S_("dense_ready"), 1)

            def head_sums(tag):
                for n in range(C1):
                    pe.wait_ge(*when(tag + "_squared", n + 1))
                    for t in range(NB):
                        ins = MM(bank(4, 1, NB * n + t), mE[:, n % 2, P * t:P * t + P], ones[:, 0:1], start=True, stop=True)
                    ins.then_inc(S_(tag + "_summed"), 1)

            def norm_sums(tag, n0, n1):
                sq = merged if tag == "n_ffn" else merged2
                for n in range(n0, n1):
                    pe.wait_ge(*when(tag + "_squared", n + 1))
                    for t in range(NB):
                        ins = MM(bank(4, 1, t), sq[:, n, P * t:P * t + P], ones[:, 0:1], start=n == t == 0,
                                 stop=n == KC - 1, skip_group_check=True)
                    ins.then_inc(S_(tag + "_summed"), 1)

            def norm_pe(tag):
                norm_sums(tag, KC - 2, KC)
                pe.wait_ge(*when(tag + "_summed", KC))
                pe.wait_ge(*when(tag + "_rms", 1))
                for t in range(NB):
                    ins = MM(bank(5, P, P * t), stat[:, 44 + t:45 + t].to_broadcast([P, P]), ident, start=True, stop=True)
                ins.then_inc(S_(tag + "_bc"), 1)

            def ada_columns(i):
                pe.wait_ge(*when("ada_summed", i + 1))
                for j in range(2):
                    ins = MM(bank(6, 1, 2 * i + j), ada_acc[i % 2][:, P * j:P * j + P], ones[:, 0:1], start=True, stop=True)
                ins.then_inc(S_("ada_used"), 1)

            def gates_rows():
                f8 = slice(0, 8)
                pe.wait_ge(*when("if_cum", 1))
                MM(bank(6)[0:4], ident[f8, 0:4], ifr[f8, 0, :], start=True, stop=False)
                MM(bank(6)[0:4], ident[f8, 4:8], ifr[f8, 3, :], start=False, stop=True)
                MM(bank(7)[0:4], ident[f8, 4:8], ifr[f8, 3, :], start=True, stop=True).then_inc(S_("if_g"), 1)

            def gates_columns():
                pe.wait_ge(*when("if_g4", 1))
                for j in range(NB):
                    ins = nc.tensor.transpose(bank(5, 4, 4 * j), ifr[0:4, 4, P * j:P * j + P], ident[0:4, 0:4])
                ins.then_inc(S_("if_cols"), 1)

            def mlstm_pe():
                pe.wait_ge(*when("if_ready", 1))
                pe.wait_ge(*when("if_negm", 1))
                pe.wait_ge(*when("mconv_silu", 8))

                def values(n):
                    h, j = n // NB, n % NB
                    pe.wait_ge(*when("ml_s", n + 1))
                    if j == 0 and h >= 2:
                        pe.wait_ge(*when("ml_h", h - 1))
                    N = S - P * j
                    MM(bank(2 + h % 2, N, P * j), vm[:, j, P * h:P * h + P], mS[:, n % 2, 0:N], start=j == 0, stop=j == NB - 1)
                    MM(bank(4 + h % 2, N, P * j), ones, mS[:, n % 2, 0:N], start=j == 0, stop=j == NB - 1
                       ).then_inc(S_("ml_pv"), 1)

                for n in range(4 * NB + 1):
                    h, j = n // NB, n % NB
                    if n < 4 * NB:
                        if j == 0:
                            sel = ident[0:4, h:h + 1].to_broadcast([4, P])
                            if h:
                                pe.wait_ge(*when("ml_m", h))
                            MM(bank(6), sel, ifr[0:4, 5, :], start=True, stop=True).then_inc(S_("ml_bc"), 1)
                        if n >= 2:
                            pe.wait_ge(*when("ml_s", n - 1))
                        N = S - P * j
                        MM(bank(n % 2, N), qkm[:, 1, h, P * j:P * j + P], qkm[:, 0, h, P * j:], start=True, stop=True
                           ).then_inc(S_("ml_qk"), 1)
                    if n >= 1:
                        values(n - 1)
                    if n < 4 * NB and j == 2:
                        sel = ident[0:4, h:h + 1].to_broadcast([4, P])
                        if h:
                            pe.wait_ge(*when("ml_h", h))
                        MM(bank(7), sel, ifr[0:4, 6, :], start=True, stop=True).then_inc(S_("ml_guard"), 1)

            def head_norm_pe(tag, free_name, free_value):
                pe.wait_ge(*when(free_name, free_value))
                head_sums(tag)
                pe.wait_ge(*when(tag + "_rms", 1))
                for c in range(C1):
                    if c >= 2:
                        pe.wait_ge(*when({"mn": "ml_gated", "dn": "df_normed"}[tag], c - 1))
                    for t in range(NB):
                        ins = MM(bank(6 + c % 2, P, P * t), rms16[:, NB * c + t:NB * c + t + 1].to_broadcast([P, P]), ident,
                                 start=True, stop=True)
                    ins.then_inc(S_(tag + "_bc"), 1)

            rms16 = small[:, 120:136]
            rms64 = small[:, 136:200]

            def qk_sums(c):
                g = ("qd", c) if c < C1 else ("kd", c - C1)
                pe.wait_ge(*when(f"bank_free{BANK[g][0]}", BANK[g][1] + 1))
                for t in range(NB):
                    ins = MM(bank(4, 2, 2 * (NB * c + t)), rt[:, c % 3, P * t:P * t + P], K("halves")[:, 0:P:DH], start=True, stop=True)
                ins.then_inc(S_("qk_summed"), 1)

            def rope_pe():
                pe.wait_ge(*when("qk_rms", 1))
                def spread(c):
                    if c >= 2:
                        pe.wait_ge(*when("qk_normed", c - 1))
                    for t in range(NB):
                        for j in range(2):
                            r1 = rms64[:, 2 * (NB * c + t) + j:2 * (NB * c + t) + j + 1].to_broadcast([P, DH])
                            ins = MM(bank(5 + 2 * (c % 2), P, P * t)[DH * j:DH * j + DH], r1, ident, start=True, stop=True)
                    ins.then_inc(S_("qk_bc"), 1)

                spread(0)
                for c in range(8):
                    if c < 7:
                        spread(c + 1)
                    pe.wait_ge(*when("qk_normed", c + 1))
                    if c >= 2:
                        pe.wait_ge(*when("qk_swapped", c - 1))
                    MM(bank(6 - 2 * (c % 2)), K("rope_swap"), qkd[:, c // C1, c % C1, :], start=True, stop=True
                       ).then_inc(S_("qk_swap"), 1)
                pe.wait_ge(*when("qk_roped", 8))

            def diff_pe():
                N = 4 * NB
                for n in range(N + 3):
                    if n < N:
                        h, i = n // NB, n % NB
                        if n >= 2:
                            pe.wait_ge(*when("df_exp", 2 * n - 2))
                        for m in range(2):
                            half = slice(DH * m, DH * m + DH)
                            b = 2 * (n % 2) + m
                            MM(bank(b, P * (i + 1)), qkd[half, 0, h, P * i:P * i + P], qkd[half, 1, h, 0:P * (i + 1)], start=True, stop=False)
                            ins = MM(bank(b, P, P * i), identb, maskb, start=False, stop=True)
                        ins.then_inc(S_("df_qk"), 1)
                    m = n - 2
                    if 0 <= m < N:
                        pe.wait_ge(*when("df_p", m + 1))
                        if m >= 2:
                            pe.wait_ge(*when("df_pt_copied", m - 1))
                        for j in range(m % NB + 1):
                            ins = nc.tensor.transpose(bank(4 + m % 2, P, P * j), dP[:, m % 2, 0, P * j:P * j + P], ident)
                        ins.then_inc(S_("df_pt"), 1)
                    m = n - 3
                    if m >= 0:
                        h, i = m // NB, m % NB
                        pe.wait_ge(*when("df_pt_copied", m + 1))
                        if i == 0 and h >= 2:
                            pe.wait_ge(*when("df_out", h - 1))
                        for j in range(i + 1):
                            ins = MM(bank(6 + h % 2, P, P * i), vd[:, j, P * h:P * h + P], dPT[:, m % 2, P * j:P * j + P],
                                     start=j == 0, stop=j == i)
                        ins.then_inc(S_("df_pv"), 1)

            def softmax_pe(tag):
                units = units_of[tag]
                N = len(units)
                for n in range(N + 3):
                    if n < N:
                        u = units[n]
                        if n >= 2:
                            pe.wait_ge(*when(tag + "_scored", n - 1))
                        o, L = 1024 * (n % 2), u["L"]
                        cuts = [(0, min(L, 512))] + ([(512, L)] if L > 512 else [])
                        for lo, hi in cuts:
                            m = u["mask"]
                            masked = m is not None and hi > m
                            ins = MM(psum[:, o + lo:o + hi], u["q"], u["k"][:, lo:hi], start=True, stop=not masked)
                            if masked:
                                b = max(lo, m)
                                ins = MM(psum[:, o + b:o + hi], identb, maskb[:, b - m:hi - m], start=False, stop=True)
                        ins.then_inc(S_(tag + "_qk"), 1)
                    m = n - 2
                    if 0 <= m < N:
                        u = units[m]
                        pe.wait_ge(*when(tag + "_p", m + 1))
                        if m >= 1:
                            pe.wait_ge(*when(tag + "_pt_copied", m))
                        for j, (lo, v) in enumerate(u["values"]):
                            ins = nc.tensor.transpose(psum[:, 2048 + P * j:2048 + P * j + P], Sb[:, m % 4, lo:lo + P], ident)
                        ins.then_inc(S_(tag + "_pt"), 1)
                    m = n - 3
                    if m >= 0:
                        u = units[m]
                        pe.wait_ge(*when(tag + "_pt_copied", m + 1))
                        if m % 8 == 0 and u["pair"] >= 2:
                            pe.wait_ge(*when(tag + "_out", u["pair"] - 1))
                        o = 512 * (6 + u["pair"] % 2) + P * u["i"]
                        dst = psum[DH * u["side"]:DH * u["side"] + DH, o:o + P]
                        for j, (lo, v) in enumerate(u["values"]):
                            kk = v.shape[0]
                            ins = MM(dst, v, PT[0:kk, m % 2, P * j:P * j + P], start=j == 0, stop=j == len(u["values"]) - 1)
                        ins.then_inc(S_(tag + "_pv"), 1)

            def ranks():
                pe.wait_ge(*when("choices", 1))
                for t in range(NB):
                    for b in range(t + 1):
                        MM(bank(7, NE, NE * t), K("strict") if b == t else ones, both[:, b, :], start=b == 0, stop=b == t)
                for b in range(NB):
                    ins = MM(bank(7, NE, NE * NB), ones, both[:, b, :], start=b == 0, stop=b == NB - 1)
                ins.then_inc(S_("rank_mm"), 1)

            na, nb = sum(n for _, n in ROWS_A), sum(n for _, n in ROWS_B)
            pe.wait_ge(*when("cst_landed", 16))
            pe.wait_ge(*when("rows_landed", 16 * len(ROWS_A)))
            nc.tensor.transpose(bank(7, na), rowsA[0:na], ident[0:na, 0:na]).then_inc(S_("col_mm"), 1)
            pe.wait_ge(*when("cols", 1))
            for u in range(2 * NB):
                t, half = u // 2, u % 2
                pe.wait_ge(*when("xs_ready", 5))
                if u >= 2:
                    pe.wait_ge(*when("xt_copied", u - 1))
                    pe.wait_ge(*when("un_ready", u - 1))
                for j in range(4):
                    c = 4 * half + j
                    i1 = nc.tensor.transpose(bank(4 + u % 2, P, P * j), xin[:, t, P * c:P * c + P], ident)
                i1.then_inc(S_("xt_ready"), 1)
                for j in range(4):
                    c = 4 * half + j
                    i2 = nc.tensor.transpose(bank(6 + u % 2, P, P * j), xs[:, t, P * c:P * c + P], ident)
                i2.then_inc(S_("us_ready"), 1)
            pe.wait_ge(*when("xt_copied", 8))
            for c in range(KC):
                i1 = nc.tensor.transpose(bank(4, M, M * c), xms[0:M, P * c:P * c + P], ident[0:M, 0:M])
            i1.then_inc(S_("um_mm"), 1)
            pe.wait_ge(*when("ul_ready", 8))
            pe.wait_ge(*when("uml_ready", 1))
            pe.wait_ge(*when("pool_set", 7))
            pe.wait_ge(*when("identb_ready", 1))

            pending = []

            def columns_of_pending():
                while pending:
                    ada_columns(pending.pop(0))

            for s in SLABS:
                name = s["name"]
                k = name[0]
                if s["kind"] == "A":
                    pending.append(name[1])
                    continue
                if name == ("ffo", 0):
                    columns_of_pending()
                    pe.wait_ge(*when("mod_ready", 1))
                if name == ("ffg", 0):
                    norm_pe("n_ffn")
                if name == ("if", 0):
                    for b in range(8):
                        pe.wait_ge(*when(f"bank_free{b}", BANK[("ffo", b)][1] + 1))
                    for n in range(KC):
                        pe.wait_ge(*when("n_fin_squared", n + 1))
                        for t in range(NB):
                            ins = MM(bank(4, 2, 2 * t), ntmp[:, n % 2, P * t:P * t + P], wsq[:, n, :], start=n == t == 0,
                                     stop=n == KC - 1, skip_group_check=True)
                        ins.then_inc(S_("n_fin_summed"), 1)
                    for tag, b, c0 in (("n_fin", 5, 44), ("n_one", 7, 56)):
                        pe.wait_ge(*when(tag + "_rms", 1))
                        for t in range(NB):
                            ins = MM(bank(b, P, P * t), stat[:, c0 + t:c0 + t + 1].to_broadcast([P, P]), ident, start=True, stop=True)
                        ins.then_inc(S_(tag + "_bc"), 1)
                    pe.wait_ge(*when("lam_prod", 2))
                    for j in range(2):
                        MM(bank(6, 1, j), small[0:DH, 68 + j:69 + j].to_broadcast([DH, P]), ones[0:DH, 0:1],
                           start=True, stop=True).then_inc(S_("lam_sums"), 1)
                    pe.wait_ge(*when("lam_exps", 1))
                if k == "branch":
                    pe.wait_ge(*when("m1_ol", name[1] + 1))
                if k == "branch2":
                    pe.wait_ge(*when("m2_ol", name[1] + 1))
                if k == "ffo":
                    i = name[1]
                    pe.wait_ge(*when("lo_ready", s["h"] + 1))
                    if i == 0:
                        pe.wait_ge(*when("f_lo", FC))
                        for c in range(4):
                            pe.wait_ge(*when(f"bank_free{c}", BANK[("ffo", c)][1]))
                    wh = WH[:, s["h"] % HL, :].rearrange("p (k n) -> p k n", k=2)
                    wl = WL[:, s["h"] % HL, :].rearrange("p (k n) -> p k n", k=2)
                    for c in range(KC):
                        for j in range(2):
                            kk = 2 * i + j
                            ins = split3(bank(c), wh[:, j, P * c:P * c + P], wl[:, j, P * c:P * c + P], FH[:, kk, :], FL_[:, kk, :],
                                         kk == 0, kk == FC - 1)
                        if i == FC // 2 - 1:
                            ins.then_inc(S_("dense_ready"), 1)
                    if i < FC // 2 - 1:
                        ins.then_inc(S_("ffo_used"), 1)
                    continue
                slab(s)
                if k in ("ffg", "ffu"):
                    columns_of_pending()
                if k in ("wo", "wo2") and name[1]:
                    norm_sums("n_ffn" if k == "wo" else "n_two", 2 * name[1] - 2, 2 * name[1])
                if k in ("qd", "kd"):
                    for c in range(2):
                        qk_sums(2 * name[1] + c + (C1 if k == "kd" else 0))
                if name == ("qm", 0):
                    gates_rows()
                if name == ("qm", 1):
                    pe.wait_ge(*when("h_final", KC))
                    gates_columns()
                if name == ("vd", 1):
                    for b in range(4):
                        pe.wait_ge(*when(f"bank_free{b}", max(BANK[g][1] + 1 for g in GROUPS if BANK[g][0] == b and GROUPS[g] <= GROUPS[s["outs"][-1]])))
                    rope_pe()
                    mlstm_pe()
                    head_norm_pe("mn", "ml_h", C1)
                    pe.wait_ge(*when("ml_gated", C1))
                    diff_pe()
                    head_norm_pe("dn", "df_out", C1)
                    pe.wait_ge(*when("df_normed", C1))
                if name == ("xc", 0):
                    pe.wait_ge(*when("params", PARAMS))
                    nc.tensor.transpose(bank(5, nb), rowsB[0:nb], ident[0:nb, 0:nb]).then_inc(S_("col_b_mm"), 1)
                    for h in range(8):
                        if h >= 2:
                            pe.wait_ge(*when("stage_ready", h - 1))
                        MM(bank(6 + h % 2, SKEW), rel[0:32, h:h + 1].to_broadcast([32, P]), K("onehot")[0:32, :], start=True,
                           stop=True).then_inc(S_("dist_mm"), 1)
                if name in LRU_AFTER:
                    c = LRU_AFTER.index(name)
                    pe.wait_ge(*when("stage_ready", 8))
                    pe.wait_ge(*when("bd_landed", 16 * 4))
                    pe.wait_ge(*when("conv_ready", c + 1))
                    if c:
                        pe.wait_ge(*when("lru_psum_read", c))
                    for g in range(2):
                        for lo, hi in ((0, 512), (512, T)):
                            ins = MM(psum[:, 2048 + 1024 * g + lo:2048 + 1024 * g + hi], bd[:, g, c, :], cv[:, c, lo:hi],
                                     start=True, stop=True)
                    ins.then_inc(S_("lru_mm"), 1)
                if name == ("qf", 1):
                    pe.wait_ge(*when("cum_ready", 2))
                    pe.wait_ge(*when("lru_psum_read", C1))
                    for h in range(8):
                        if h >= 2:
                            pe.wait_ge(*when("cum_copied", h - 1))
                        for lo, hi in ((0, 512), (512, T)):
                            o = 2048 + 1024 * (h % 2)
                            ins = MM(psum[:, o + lo:o + hi], ident[0:8, h:h + 1].to_broadcast([8, P]), fl4[0:8, 2, lo:hi],
                                     start=True, stop=True)
                        ins.then_inc(S_("cum_rows"), 1)
                    pe.wait_ge(*when("cum_copied", 8))
                    for g in s["outs"]:
                        pe.wait_ge(*when(f"bank_free{BANK[g][0]}", BANK[g][1] + 1))
                    for b in range(4):
                        pe.wait_ge(*when(f"bank_free{b}", max(BANK[g][1] + 1 for g in GROUPS if BANK[g][0] == b and GROUPS[g] <= GROUPS[s["outs"][-1]])))
                    softmax_pe("fox")
                    pe.wait_ge(*when("fox_scored", 32))
                if name == ("kava", 0):
                    pe.wait_ge(*when("fox_out", 4))
                    for b in range(4):
                        pe.wait_ge(*when(f"bank_free{b}", max(BANK[g][1] + 1 for g in GROUPS if BANK[g][0] == b and GROUPS[g] <= GROUPS[s["outs"][-1]])))
                    softmax_pe("swa")
                    pe.wait_ge(*when("swa_scored", 32))
            norm_pe("n_two")
            pe.wait_ge(*when("router_landed", 32))
            for c in range(KC):
                pe.wait_ge(*when("h2_ready", c + 1))
                ins = MM(bank(6)[0:NG + NE], wr[:, c, :], H2[:, c, :], start=c == 0, stop=c == KC - 1)
            ins.then_inc(S_("router_mm"), 1)
            pe.wait_ge(*when("logits_copied", 1))
            for t in range(NB):
                ins = nc.tensor.transpose(bank(5, NG + NE, (NG + NE) * t), lgT[0:NG + NE, P * t:P * t + P],
                                          ident[0:NG + NE, 0:NG + NE])
            ins.then_inc(S_("logits_ready"), 1)

            def token_major(v, src):
                t, half = v // 2 % NB, v % 2
                for j in range(4):
                    ins = nc.tensor.transpose(bank(v % 4, P, P * j), src[:, 4 * half + j, P * t:P * t + P], ident)
                ins.then_inc(S_("token_major"), 1)

            for v in range(2 * NB):
                if v >= 4:
                    pe.wait_ge(*when("h2t_odd" if v % 2 else "h2t_even", v // 2 - 1))
                if v == 4:
                    ranks()
                token_major(v, H2)
            for v in range(2 * NB):
                if v < 4:
                    pe.wait_ge(*when("h2t_odd" if v % 2 else "h2t_even", NB - 1 + v // 2))
                else:
                    pe.wait_ge(*when("xtm_odd" if v % 2 else "xtm_even", v // 2 - 1))
                token_major(2 * NB + v, hT)
            for c in range(KC):
                ins = MM(bank(4 + c // 4, P, P * (c % 4)), gate2[:, c:c + 1].to_broadcast([P, P]), ident, start=True, stop=True)
            ins.then_inc(S_("g2_mm"), 1)
            pe.wait_ge(*when("xtm_even", NB))
            pe.wait_ge(*when("xtm_odd", NB))
            pe.wait_ge(*when("g2_even", 1))
            pe.wait_ge(*when("g2_odd", 1))

            def transpose_rows(i, u):
                n = UN * i + u
                pe.wait_ge(*when(f"xg_landed{u}", 16 * i + 16))
                if not (isinstance(i, int) and n == 0):
                    pe.wait_ge(*when("xt_even", n))
                    pe.wait_ge(*when("xt_odd", n))
                for j in range(KC):
                    ins = nc.tensor.transpose(bank(j // 4, P, P * (j % 4)), Xg[:, u, P * j:P * j + P], ident)
                ins.then_inc(S_("tx_done"), 1)

            def transpose_act(i, u):
                n = UN * i + u
                pe.wait_ge(*when("act_ready", n + 1))
                if not (isinstance(i, int) and n == 0):
                    pe.wait_ge(*when("at_ready", n))
                for j in range(2):
                    ins = nc.tensor.transpose(bank(2, P, P * j), sA[:, u, P * j:P * j + P], ident)
                ins.then_inc(S_("ta_done"), 1)

            def gate_up(i, u):
                n = UN * i + u
                pe.wait_ge(*when(f"gu_landed{u}", 32 * i + 32))
                pe.wait_ge(*when("xt_even", n + 1))
                pe.wait_ge(*when("xt_odd", n + 1))
                for k in range(KC):
                    ins = MM(bank(3), XT[:, u, P * k:P * k + P], WE[:, u, 2 * DE * k:2 * DE * k + 2 * DE], start=k == 0, stop=k == KC - 1)
                ins.then_inc(S_("gu_done"), 1)

            def down(i, u):
                n = UN * i + u
                pe.wait_ge(*when(f"down_landed{u}", 16 * i + 16))
                pe.wait_ge(*when("at_ready", n + 1))
                if not (isinstance(i, int) and n == 0):
                    pe.wait_ge(*when("y_even", n))
                    pe.wait_ge(*when("y_odd", n))
                for half in range(2):
                    for j in range(2):
                        o = 2 * DE * KC + D * j + 512 * half
                        ins = MM(bank(4 + half), AT[:, u, P * j:P * j + P], WE[:, u, o:o + 512], start=j == 0, stop=j == 1)
                ins.then_inc(S_("y_done"), 1)

            transpose_rows(0, 0)
            def step(i, u, ahead, before):
                if ahead:
                    transpose_rows(*ahead)
                if before:
                    transpose_act(*before)
                gate_up(i, u)
                if before:
                    down(*before)

            run_tiles(pe, step)
            transpose_act(TURNS - 1, UN - 1)
            down(TURNS - 1, UN - 1)
            with pe.If(more_tiles(pe)):
                transpose_rows(TURNS, 0)
                run_overflow(step)
                transpose_act(NT // UN - 1, UN - 1)
                down(NT // UN - 1, UN - 1)


def kernel(**inputs):
    import concourse.bacc as bacc
    from concourse.bass_utils import run_bass_kernel_spmd

    arrays = {name: np.ascontiguousarray(value) for name, value in inputs.items()}
    arrays["const"] = constants()
    nc = bacc.Bacc("TRN2", target_bir_lowering=False, num_devices=1)
    views = {name: nc.dram_tensor(name, value.shape, mybir.dt.from_np(value.dtype), kind="ExternalInput").ap()
             for name, value in arrays.items()}
    out = nc.dram_tensor("out", (1, S, D), F32, kind="ExternalOutput").ap()
    build_program(nc, views, out)
    result = run_bass_kernel_spmd(nc, [arrays], core_ids=[0])
    return result.results[0]["out"]
```
